# Optimizing a Trainium2 kernel written in Bass

```python
import math
import jax
import jax.numpy as jnp
from jax import lax
import numpy as np

D_MODEL = 1024
BATCH = 1
SEQ = 1024
DEPTH = 2

HEAD_DIM = 64
FOX_HEADS = 8
DIFF_HEADS = 4
DIFF_V_DIM = 2 * HEAD_DIM
FOX_WIDTH = FOX_HEADS * HEAD_DIM
DIFF_QK_WIDTH = DIFF_HEADS * 2 * HEAD_DIM
DIFF_WIDTH = DIFF_HEADS * DIFF_V_DIM
ATTN_WIDTH = FOX_WIDTH + DIFF_WIDTH
ATTN_SPLITS = (FOX_WIDTH, FOX_WIDTH, FOX_WIDTH, FOX_HEADS, DIFF_QK_WIDTH, DIFF_QK_WIDTH, DIFF_WIDTH, ATTN_WIDTH)
ATTN_IN = 3 * FOX_WIDTH + FOX_HEADS + 2 * DIFF_QK_WIDTH + DIFF_WIDTH + ATTN_WIDTH

ML_HEADS = 8
ML_QK_DIM = 64
ML_V_DIM = 128
ML_QK_WIDTH = ML_HEADS * ML_QK_DIM
ML_WIDTH = ML_HEADS * ML_V_DIM
ML_SPLITS = (ML_QK_WIDTH, ML_QK_WIDTH, ML_WIDTH, ML_HEADS, ML_HEADS, ML_WIDTH, ML_WIDTH)
ML_IN = 2 * ML_QK_WIDTH + 3 * ML_WIDTH + 2 * ML_HEADS

Q_BLOCK = 128
ML_CHUNK = 128
ROPE_THETA = 10000.0
EPS = 1e-6
POS_OFFSET_MAX = 4096
N_ATTN_LAYERS = (DEPTH + 1) // 2
N_MLSTM_LAYERS = DEPTH // 2

kernel_name = 'hybrid_fox_diff_mlstm'

F32 = jnp.float32

def rms_norm(x, g):
    xf = x.astype(F32)
    y = xf * lax.rsqrt(jnp.mean(xf * xf, axis=-1, keepdims=True) + EPS)
    return (y * g.astype(F32)).astype(x.dtype)

def split_cols(t, sizes):
    idx = np.cumsum(sizes)[:-1].tolist()
    return jnp.split(t, idx, axis=-1)

def rope(x, pos):
    half = x.shape[-1] // 2
    inv = ROPE_THETA ** (-jnp.arange(half, dtype=F32) / half)
    ang = pos.astype(F32)[..., None] * inv
    ang = ang.reshape((x.shape[0],) + (1,) * (x.ndim - 3) + ang.shape[1:])
    cos, sin = jnp.cos(ang), jnp.sin(ang)
    x1 = x[..., :half].astype(F32)
    x2 = x[..., half:].astype(F32)
    return jnp.concatenate([x1 * cos - x2 * sin, x1 * sin + x2 * cos], axis=-1).astype(x.dtype)

def seq_blocks(t, axis, size):
    n = t.shape[axis] // size
    t = t.reshape(t.shape[:axis] + (n, size) + t.shape[axis + 1:])
    return jnp.moveaxis(t, axis, 0)

def seq_unblocks(t, axis):
    t = jnp.moveaxis(t, 0, axis)
    return t.reshape(t.shape[:axis] + (-1,) + t.shape[axis + 2:])

def fox_attention(q, k, v, log_f):
    S = q.shape[2]
    scale = HEAD_DIM ** -0.5
    F = jnp.cumsum(log_f, axis=-1)
    key_pos = jnp.arange(S)
    nb = S // Q_BLOCK

    def block(args):
        i, qi, Fi = args
        q_pos = i * Q_BLOCK + jnp.arange(Q_BLOCK)
        s = jnp.einsum('bhqd,bhkd->bhqk', qi, k, preferred_element_type=F32) * scale
        s = s + Fi[..., :, None] - F[..., None, :]
        s = jnp.where(key_pos[None, :] <= q_pos[:, None], s, -jnp.inf)
        p = jax.nn.softmax(s, axis=-1)
        return jnp.einsum('bhqk,bhkd->bhqd', p.astype(v.dtype), v)

    out = lax.map(block, (jnp.arange(nb), seq_blocks(q, 2, Q_BLOCK), seq_blocks(F, 2, Q_BLOCK)))
    return seq_unblocks(out, 2)

def diff_attention(q, k, v, lam):
    S = q.shape[3]
    scale = HEAD_DIM ** -0.5
    key_pos = jnp.arange(S)
    nb = S // Q_BLOCK

    def block(args):
        i, qi = args
        q_pos = i * Q_BLOCK + jnp.arange(Q_BLOCK)
        s = jnp.einsum('bhcqd,bhckd->bhcqk', qi, k, preferred_element_type=F32) * scale
        s = jnp.where(key_pos[None, :] <= q_pos[:, None], s, -jnp.inf)
        p = jax.nn.softmax(s, axis=-1)
        pd = p[:, :, 0] - lam * p[:, :, 1]
        return jnp.einsum('bhqk,bhke->bhqe', pd.astype(v.dtype), v)

    out = lax.map(block, (jnp.arange(nb), seq_blocks(q, 3, Q_BLOCK)))
    return seq_unblocks(out, 2)

def mlstm_chunkwise(q, k, v, log_i, log_f):
    B, H, S, dk = q.shape
    dv = v.shape[-1]
    L = ML_CHUNK
    causal = jnp.tril(jnp.ones((L, L), dtype=bool))

    def step(carry, xs):
        C, n, m = carry
        qi, ki, vi, li, lf = xs
        qf, kf, vf = qi.astype(F32), ki.astype(F32), vi.astype(F32)
        b = jnp.cumsum(lf, axis=-1)
        a = b[..., -1]
        log_d = b[..., :, None] - b[..., None, :] + li[..., None, :]
        log_d = jnp.where(causal, log_d, -jnp.inf)
        log_inter = b + m[..., None]
        m_t = jnp.maximum(log_inter, jnp.max(log_d, axis=-1))
        d = jnp.exp(log_d - m_t[..., None])
        w_inter = jnp.exp(log_inter - m_t)
        s = jnp.einsum('bhtd,bhsd->bhts', qf, kf) * d
        num = w_inter[..., None] * jnp.einsum('bhtd,bhde->bhte', qf, C) + jnp.einsum('bhts,bhse->bhte', s, vf)
        den = w_inter * jnp.einsum('bhtd,bhd->bht', qf, n) + jnp.sum(s, axis=-1)
        h = num / jnp.maximum(jnp.abs(den), jnp.exp(-m_t))[..., None]
        g = a[..., None] - b + li
        m_new = jnp.maximum(a + m, jnp.max(g, axis=-1))
        w_old = jnp.exp(a + m - m_new)
        w_s = jnp.exp(g - m_new[..., None])
        C_new = w_old[..., None, None] * C + jnp.einsum('bhs,bhsd,bhse->bhde', w_s, kf, vf)
        n_new = w_old[..., None] * n + jnp.einsum('bhs,bhsd->bhd', w_s, kf)
        return (C_new, n_new, m_new), h.astype(v.dtype)

    init = (jnp.zeros((B, H, dk, dv), F32), jnp.zeros((B, H, dk), F32), jnp.zeros((B, H), F32))
    xs = (seq_blocks(q, 2, L), seq_blocks(k, 2, L), seq_blocks(v, 2, L),
          seq_blocks(log_i, 2, L), seq_blocks(log_f, 2, L))
    _, hs = lax.scan(step, init, xs)
    return seq_unblocks(hs, 2)

def attention_layer(x, pos, norm_g, w_in, b_f, lam_q1, lam_k1, lam_q2, lam_k2, subln_g, w_out, layer_idx):
    B, S, _ = x.shape
    h = rms_norm(x, norm_g)
    proj = jnp.einsum('bsd,de->bse', h, w_in)
    fq, fk, fv, ff, dq, dk, dv, z = split_cols(proj, ATTN_SPLITS)

    def heads(t, nh):
        return t.reshape(B, S, nh, -1).transpose(0, 2, 1, 3)

    log_f = jax.nn.log_sigmoid((ff + b_f).astype(F32)).transpose(0, 2, 1)
    o_fox = fox_attention(heads(fq, FOX_HEADS), heads(fk, FOX_HEADS), heads(fv, FOX_HEADS), log_f)

    dq = rope(dq.reshape(B, S, DIFF_HEADS, 2, HEAD_DIM).transpose(0, 2, 3, 1, 4), pos)
    dk = rope(dk.reshape(B, S, DIFF_HEADS, 2, HEAD_DIM).transpose(0, 2, 3, 1, 4), pos)
    lam_init = 0.8 - 0.6 * math.exp(-0.3 * layer_idx)
    lam = (jnp.exp(jnp.sum(lam_q1.astype(F32) * lam_k1.astype(F32)))
           - jnp.exp(jnp.sum(lam_q2.astype(F32) * lam_k2.astype(F32))) + lam_init)
    o_diff = diff_attention(dq, dk, heads(dv, DIFF_HEADS), lam)
    o_diff = rms_norm(o_diff, subln_g) * (1.0 - lam_init)

    y = jnp.concatenate([o_fox.transpose(0, 2, 1, 3).reshape(B, S, FOX_WIDTH),
                         o_diff.transpose(0, 2, 1, 3).reshape(B, S, DIFF_WIDTH)], axis=-1)
    y = y * jax.nn.silu(z)
    return x + jnp.einsum('bse,ed->bsd', y, w_out)

def mlstm_layer(x, norm_g, w_in, b_i, b_f, w_out):
    B, S, _ = x.shape
    h = rms_norm(x, norm_g)
    proj = jnp.einsum('bsd,de->bse', h, w_in)
    q, k, v, ig, fg, og, z = split_cols(proj, ML_SPLITS)

    def heads(t, nh):
        return t.reshape(B, S, nh, -1).transpose(0, 2, 1, 3)

    q = heads(q, ML_HEADS)
    k = heads(k, ML_HEADS) * (ML_QK_DIM ** -0.5)
    v = heads(v, ML_HEADS)
    log_i = (ig + b_i).astype(F32).transpose(0, 2, 1)
    log_f = jax.nn.log_sigmoid((fg + b_f).astype(F32)).transpose(0, 2, 1)
    hm = mlstm_chunkwise(q, k, v, log_i, log_f)
    hm = hm.transpose(0, 2, 1, 3).reshape(B, S, ML_WIDTH)
    y = jax.nn.sigmoid(og) * hm * jax.nn.silu(z)
    return x + jnp.einsum('bse,ed->bsd', y, w_out)

def setup_inputs(seed: int = 0) -> dict:
    key = jax.random.key(seed)
    ks = jax.random.split(key, 18)
    ne, no = N_ATTN_LAYERS, N_MLSTM_LAYERS
    nrm = jax.random.normal
    x = nrm(ks[0], (BATCH, SEQ, D_MODEL), F32)
    positions = (jnp.arange(SEQ, dtype=jnp.int32)[None, :]
                 + jax.random.randint(ks[1], (BATCH, 1), 0, POS_OFFSET_MAX, dtype=jnp.int32))
    attn_norm_g = 1.0 + 0.02 * nrm(ks[2], (ne, D_MODEL), F32)
    attn_w_in = nrm(ks[3], (ne, D_MODEL, ATTN_IN), F32) * D_MODEL ** -0.5
    fox_b_f = jax.random.uniform(ks[4], (ne, FOX_HEADS), F32, 1.0, 4.0)
    diff_lam_q1 = 0.1 * nrm(ks[5], (ne, HEAD_DIM), F32)
    diff_lam_k1 = 0.1 * nrm(ks[6], (ne, HEAD_DIM), F32)
    diff_lam_q2 = 0.1 * nrm(ks[7], (ne, HEAD_DIM), F32)
    diff_lam_k2 = 0.1 * nrm(ks[8], (ne, HEAD_DIM), F32)
    diff_subln_g = 1.0 + 0.02 * nrm(ks[9], (ne, DIFF_V_DIM), F32)
    attn_w_out = nrm(ks[10], (ne, ATTN_WIDTH, D_MODEL), F32) * ATTN_WIDTH ** -0.5
    ml_norm_g = 1.0 + 0.02 * nrm(ks[11], (no, D_MODEL), F32)
    ml_w_in = nrm(ks[12], (no, D_MODEL, ML_IN), F32) * D_MODEL ** -0.5
    ml_b_i = 0.1 * nrm(ks[13], (no, ML_HEADS), F32)
    ml_b_f = jax.random.uniform(ks[14], (no, ML_HEADS), F32, 3.0, 6.0)
    ml_w_out = nrm(ks[15], (no, ML_WIDTH, D_MODEL), F32) * ML_WIDTH ** -0.5
    final_norm_g = 1.0 + 0.02 * nrm(ks[16], (D_MODEL,), F32)
    return {'x': x, 'positions': positions, 'attn_norm_g': attn_norm_g, 'attn_w_in': attn_w_in,
            'fox_b_f': fox_b_f, 'diff_lam_q1': diff_lam_q1, 'diff_lam_k1': diff_lam_k1,
            'diff_lam_q2': diff_lam_q2, 'diff_lam_k2': diff_lam_k2, 'diff_subln_g': diff_subln_g,
            'attn_w_out': attn_w_out, 'ml_norm_g': ml_norm_g, 'ml_w_in': ml_w_in, 'ml_b_i': ml_b_i,
            'ml_b_f': ml_b_f, 'ml_w_out': ml_w_out, 'final_norm_g': final_norm_g}

def reference(x, positions, attn_norm_g, attn_w_in, fox_b_f, diff_lam_q1, diff_lam_k1, diff_lam_q2,
              diff_lam_k2, diff_subln_g, attn_w_out, ml_norm_g, ml_w_in, ml_b_i, ml_b_f, ml_w_out,
              final_norm_g):
    for layer in range(DEPTH):
        j = layer // 2
        if layer % 2 == 0:
            x = attention_layer(x, positions, attn_norm_g[j], attn_w_in[j], fox_b_f[j],
                                diff_lam_q1[j], diff_lam_k1[j], diff_lam_q2[j], diff_lam_k2[j],
                                diff_subln_g[j], attn_w_out[j], layer)
        else:
            x = mlstm_layer(x, ml_norm_g[j], ml_w_in[j], ml_b_i[j], ml_b_f[j], ml_w_out[j])
    return rms_norm(x, final_norm_g)


_drawn_inputs = setup_inputs


def setup_inputs(seed=0):
    import zlib

    import numpy as np

    out = dict(_drawn_inputs(seed))
    spreads = {}
    factors = {'diff_lam_q1': 8.0, 'ml_b_i': 2.761, 'final_norm_g': 2.861}
    for name, (base, spread) in spreads.items():
        noise = np.random.default_rng([zlib.crc32(name.encode()), seed]).standard_normal(out[name].shape)
        drawn = base * np.exp(spread * noise) if base else spread * noise
        out[name] = jnp.asarray(drawn.astype(out[name].dtype))
    for name, factor in factors.items():
        out[name] = (out[name] * factor).astype(out[name].dtype)
    return out
```

```python
import math
from contextlib import ExitStack

import numpy as np

import concourse.bass as bass
from concourse import mybir

F32 = mybir.dt.float32
F32R = mybir.dt.float32r
I32 = mybir.dt.int32
ALU = mybir.AluOpType
ACT = mybir.ActivationFunctionType
AX = mybir.AxisListType

P = 128
SEQ = 1024
D_MODEL = 1024
NT = SEQ // P
NK = D_MODEL // P
PANEL = 512
RING = 4

HEAD_DIM = 64
FOX_HEADS = 8
DIFF_HEADS = 4
FOX_WIDTH = FOX_HEADS * HEAD_DIM
DIFF_WIDTH = DIFF_HEADS * 2 * HEAD_DIM
COL_FQ = 0
COL_FK = COL_FQ + FOX_WIDTH
COL_FV = COL_FK + FOX_WIDTH
COL_FF = COL_FV + FOX_WIDTH
COL_DQ = COL_FF + FOX_HEADS
COL_DK = COL_DQ + DIFF_WIDTH
COL_DV = COL_DK + DIFF_WIDTH
COL_AZ = COL_DV + DIFF_WIDTH

ML_HEADS = 8
ML_QK = 64
ML_V = 128
COL_MQ = 0
COL_MV = 2 * ML_HEADS * ML_QK
COL_MG = COL_MV + ML_HEADS * ML_V
COL_MO = COL_MG + 2 * ML_HEADS
COL_MZ = COL_MO + ML_HEADS * ML_V

EPS = 1e-6
NEG = -1.0e30
LAM_INIT = 0.8 - 0.6 * math.exp(-0.3 * 0)
TWO_PI_1 = 6.28125
TWO_PI_2 = 0.00193500518798828125
TWO_PI_3 = 2.0 * math.pi - TWO_PI_1 - TWO_PI_2
PI_SAFE = 3.1415925
ROUND = 12582912.0

PAIRS = 8
CHUNKS_V, CHUNKS_PAIRS, CHUNKS_PANEL = 2 * NK, PAIRS * 4, NK
FIRST_V = 0
FIRST_PAIRS = FIRST_V + CHUNKS_V
FIRST_Z = FIRST_PAIRS + CHUNKS_PAIRS
FIRST_O0 = FIRST_Z + 2 * NK
FIRST_A = FIRST_O0 + 2 * NK
FIRST_B = FIRST_A + 4 * NK
FIRST_O1 = FIRST_B + 4 * NK

C_IDENT, C_MASKQ, C_MASKK, C_PERM = (P * n for n in range(4))
C_INV = 4 * P
C_SIGN = C_INV + 1
C_EARLY = C_SIGN + 1
C_RESET = C_EARLY
C_COLS = C_RESET + SEQ


def constants():
    c = np.zeros((P, C_COLS), np.float32)
    i = np.arange(P)
    c[:, C_IDENT:C_IDENT + P] = np.eye(P)
    c[:, C_MASKQ:C_MASKQ + P] = np.where(i[None, :] > i[:, None], NEG, 0.0)
    c[:, C_MASKK:C_MASKK + P] = np.where(i[None, :] < i[:, None], NEG, 0.0)
    c[i, C_PERM + (i ^ 32)] = 1.0
    half = HEAD_DIM // 2
    inv = np.float32(10000.0) ** (-np.arange(half, dtype=np.float32) / np.float32(half))
    c[:, C_INV] = inv[i % half]
    c[:, C_SIGN] = np.where(i % HEAD_DIM < half, -1.0, 1.0)
    c[:, C_RESET:C_RESET + SEQ] = 1.0
    c[:, C_RESET:C_RESET + SEQ:P] = 0.0
    return c


MAX_CHUNKS = [(i, c * 4, min(i + 1 - 4 * c, 4)) for i in range(NT) for c in range(i // 4 + 1)]
EXP_CHUNKS = [(k, max(4 * g, k), 4 * g + 4) for g in range(2) for k in range(4 * g + 4)]
EXP_AT = {}
_at = 0
for _n, (_k, _a, _b) in enumerate(EXP_CHUNKS):
    EXP_AT[(_k, _a // 4)] = (_at - _a * P)
    _at += (_b - _a) * P
PT_COLS = _at


def build(nc, x, positions, attn_norm_g, attn_w_in, fox_b_f, lams, subln_g, attn_w_out,
          ml_norm_g, ml_w_in, ml_b, ml_w_out, final_norm_g, const, out):
    v_scr = nc.dram_tensor("v_scr", (SEQ, D_MODEL), F32).ap()
    o_scr = nc.dram_tensor("o_scr", (SEQ, D_MODEL), F32).ap()
    x1_scr = nc.dram_tensor("x1_scr", (SEQ, D_MODEL), F32).ap()
    m_scr = nc.dram_tensor("m_scr", (ML_HEADS, SEQ), F32).ap()
    f_scr = nc.dram_tensor("f_scr", (FOX_HEADS, 2, SEQ), F32R).ap()

    ctx = ExitStack()
    with ctx:
        def sb(name, shape, dt=F32, scope=ctx):
            return scope.enter_context(nc.sbuf_tensor(name, shape, dt))

        def sem(name):
            return ctx.enter_context(nc.semaphore(name))

        bank = ctx.enter_context(nc.psum_tensor("bank", [P, 8, PANEL], F32))

        w_raw = sb("w_raw", [P, RING, PANEL])
        w_hi = sb("w_hi", [P, RING, PANEL], F32R)
        w_lo = sb("w_lo", [P, RING, PANEL], F32R)
        ident = sb("ident", [P, P])
        perm = sb("perm", [P, P])
        ident_r = sb("ident_r", [P, P], F32R)
        mask_q = sb("mask_q", [P, P], F32R)
        mask_k = sb("mask_k", [P, P], F32R)
        gate_raw = sb("gate_raw", [P, NK, 16])
        stat = sb("stat", [P, 4, NT])
        neg_half = sb("neg_half", [P, NT])
        neg_lam = sb("neg_lam", [P, 1])
        gate_hi = sb("gate_hi", [P, NK, 16], F32R)
        gate_lo = sb("gate_lo", [P, NK, 16], F32R)
        gate_b = sb("gate_b", [8, 4])
        inv_sign = sb("inv_sign", [P, 2])

        ht_scope = ExitStack()
        ht_hi = sb("ht_hi", [P, NK, SEQ], F32R, ht_scope)
        ht_lo = sb("ht_lo", [P, NK, SEQ], F32R, ht_scope)

        att = ExitStack()
        q_a = [[sb(f"q_a{c}{a}", [P, SEQ], F32R, att) for a in range(2)] for c in range(2)]
        q_b = [[sb(f"q_b{c}{a}", [68, SEQ], F32R, att) for a in range(2)] for c in range(2)]
        k_a = [[sb(f"k_a{c}{a}", [P, SEQ], F32R, att) for a in range(2)] for c in range(2)]
        k_b = [[sb(f"k_b{c}{a}", [68, SEQ], F32R, att) for a in range(2)] for c in range(2)]
        cos_t = sb("cos_t", [P, SEQ], F32, att)
        sin_t = sb("sin_t", [P, SEQ], F32, att)
        v_pair = [sb(f"v_pair{c}", [P, NT, 130], F32, att) for c in range(2)]
        m_part = sb("m_part", [P, 2, 12], F32, att)
        m_max = sb("m_max", [P, 2, NT], F32, att)
        m_cols = sb("m_cols", [P, 2, NT, 4], F32R, att)
        recip = sb("recip", [P, 2, 16], F32, att)
        sub_g = sb("sub_g", [P, P], F32, att)
        sub_ss = sb("sub_ss", [P, 2, NT], F32, att)
        c_work = ExitStack()
        c_raw = sb("c_raw", [P, C_EARLY], F32, c_work)
        turn = sb("turn", [P, SEQ], F32, c_work)
        angle = sb("angle", [P, SEQ], F32, c_work)
        pos_i = sb("pos_i", [P, SEQ], I32, c_work)
        c_work.close()
        sub_sq = sb("sub_sq", [P, NT, P], F32, att)
        o_pair = [sb(f"o_pair{c}", [P, NT, P], F32, att) for c in range(2)]
        work = ExitStack()
        probs = sb("probs", [P, PT_COLS], F32, work)
        qs = sb("qs", [P, PANEL], F32, work)
        rot = sb("rot", [P, PANEL], F32, work)
        work.close()
        v_work = ExitStack()
        below = sb("below", [P, C_EARLY], F32, v_work)
        row = [sb(f"row{n}", [8, SEQ], F32, v_work) for n in range(2)]
        f_parts = sb("f_parts", [8, 2, SEQ], F32R, v_work)
        lam_row = sb("lam_row", [1, 4 * HEAD_DIM + 8], F32, v_work)
        v_work.close()
        att.close()

        lay = ExitStack()
        buf = [sb(f"buf{n}", [P, NT, D_MODEL], F32, lay) for n in range(2)]
        silu = sb("silu", [P, 2, PANEL], F32, lay)
        pad = sb("pad", [P, SEQ], F32, lay)
        g_rows = sb("g_rows", [P, D_MODEL], F32, lay)
        lay.close()
        vs = ExitStack()
        v_stage = sb("v_stage", [P, NT, PANEL], F32, vs)
        vs.close()

        hid = ExitStack()
        qk_rows = sb("qk_rows", [P, NT, 2 * ML_HEADS * ML_QK], F32, hid)
        v_rows = sb("v_rows", [P, NT, ML_HEADS, 130], F32, hid)
        gl = ExitStack()
        gl_rows = sb("gl_rows", [P, NT, ML_HEADS * ML_V], F32, gl)
        gl.close()
        rw = ExitStack()
        g_in = sb("g_in", [16, SEQ], F32, rw)
        gr = [sb(f"gr{n}", [8, SEQ], F32, rw) for n in range(5)]
        rows4 = sb("rows4", [P, SEQ], F32, rw)
        reset = sb("reset", [8, SEQ], F32, rw)
        rw.close()
        gap = sb("gap", [P, NT * D_MODEL], F32, hid)
        decay = [sb(f"decay{n}", [P, ML_HEADS, P], F32, hid) for n in range(3)]
        cols = sb("cols", [P, NT, 4, 8], F32, hid)
        w_old = sb("w_old", [P, NT, ML_HEADS], F32, hid)
        lrow = sb("lrow", [8, NT, 10], F32, hid)
        ones8 = sb("ones8", [8, P], F32, hid)
        zs = sb("zs", [P, 2, PANEL], F32, hid)
        hid.close()
        ht_scope.close()

        ml = ExitStack()
        q_t = [sb(f"q_t{n}", [P, 4, P], F32, ml) for n in range(2)]
        k_t = [sb(f"k_t{n}", [P, 4, P], F32, ml) for n in range(2)]
        kw = [sb(f"kw{n}", [P, ML_HEADS, ML_QK], F32, ml) for n in range(2)]
        qd_t = [sb(f"qd_t{n}", [P, 4, P], F32, ml) for n in range(2)]
        q_decayed = sb("q_decayed", [P, ML_HEADS, ML_QK], F32, ml)
        sd = [sb(f"sd{n}", [P, 4, P], F32, ml) for n in range(4)]
        state = sb("state", [P, 4, 130], F32, ml)
        den = sb("den", [P, 2, 3, 2, 2], F32, ml)
        ml.close()

        raw_loaded = [sem(f"raw_loaded{n}") for n in range(RING)]
        v_stored = [sem(f"v_stored{n}") for n in range(NT)]
        v_loaded = [sem(f"v_loaded{n}") for n in range(2)]
        o_stored = [sem(f"o_stored{n}") for n in range(2)]
        tile_loaded = [sem(f"tile_loaded{n}") for n in range(NT)]
        hi_split = sem("hi_split")
        w_ready = sem("w_ready")
        w_used = sem("w_used")
        acc_ready = sem("acc_ready")
        bank_free = sem("bank_free")
        turned = sem("turned")
        turned_hi = sem("turned_hi")
        turned_lo = sem("turned_lo")
        consts_loaded = sem("consts_loaded")
        consts_ready = sem("consts_ready")
        squares_ready = sem("squares_ready")
        mean_ready = sem("mean_ready")
        rstd_ready = sem("rstd_ready")
        xn_ready = sem("xn_ready")
        g_loaded = sem("g_loaded")
        small_loaded = sem("small_loaded")
        gate_acc = sem("gate_acc")
        dve_chain = sem("dve_chain")
        pool_chain = sem("pool_chain")
        gate_e = sem("gate_e")
        gate_u = sem("gate_u")
        gate_l = sem("gate_l")
        f_ready = sem("f_ready")
        f_stored = sem("f_stored")
        rowf_loaded = sem("rowf_loaded")
        pos_loaded = sem("pos_loaded")
        rope_args = sem("rope_args")
        rope_ready = sem("rope_ready")
        lam_loaded = sem("lam_loaded")
        lam_sum = sem("lam_sum")
        gate_split = sem("gate_split")
        lam_exp = sem("lam_exp")
        lam_one = sem("lam_one")
        lam_bc = sem("lam_bc")
        lam_ready = sem("lam_ready")
        proj_done = sem("proj_done")
        pj_copied = sem("pj_copied")
        pj_free = sem("pj_free")
        perm_done = sem("perm_done")
        roped = sem("roped")
        qk_hi = sem("qk_hi")
        qk_ready = sem("qk_ready")
        qk_twice = sem("qk_twice")
        max_in = sem("max_in")
        max_done = sem("max_done")
        m_ready = sem("m_ready")
        m_turned = sem("m_turned")
        m_rows = sem("m_rows")
        exp_in = sem("exp_in")
        probs_ready = sem("probs_ready")
        pv_ready = sem("pv_ready")
        pv_free = sem("pv_free")
        o_loaded = [sem(f"o_loaded{n}") for n in range(NT)]
        x_again = [sem(f"x_again{n}") for n in range(NT)]
        o_squares = sem("o_squares")
        helper_init = sem("helper_init")
        y_ready = sem("y_ready")
        x1_stored = sem("x1_stored")
        gate_moved = sem("gate_moved")
        gate_in = sem("gate_in")
        cols_turned = sem("cols_turned")
        cols_ready = sem("cols_ready")
        wold_bc = sem("wold_bc")
        ml_loaded = sem("ml_loaded")
        ml_init = sem("ml_init")
        gate_exp = sem("gate_exp")
        gate_ln = sem("gate_ln")
        helper_sub = sem("helper_sub")
        q_turned = sem("q_turned")
        k_turned = sem("k_turned")
        q_ready = sem("q_ready")
        k_ready = sem("k_ready")
        s_in = sem("s_in")
        neg_ready = sem("neg_ready")
        m_stored = sem("m_stored")
        m_loaded = [sem(f"m_loaded{n}") for n in range(3)]
        qd_ready = sem("qd_ready")
        qd_turned = sem("qd_turned")
        qd_copied = sem("qd_copied")
        kw_ready = sem("kw_ready")
        mask_ready = sem("mask_ready")
        d_ready = sem("d_ready")
        sd_ready = sem("sd_ready")
        inter_in = sem("inter_in")
        state_ready = sem("state_ready")
        out_stored = sem("out_stored")
        g1_loaded = sem("g1_loaded")
        g2_loaded = sem("g2_loaded")
        gl_ready = sem("gl_ready")

        def panels(e, n, body):
            if n > 2:
                with e.Fori(0, n) as p:
                    body(p)
            else:
                for p in range(n):
                    body(p)

        chunk_used, used = [], 0
        for n in range(FIRST_O1 + 2 * NK):
            if FIRST_PAIRS <= n < FIRST_Z:
                last = n % 2 == 1
                signal = (proj_done, 2 * ((n - FIRST_PAIRS) // 2 + 1))
            else:
                last = n % NK == NK - 1
                done = n + 1 if n < FIRST_PAIRS else n + 1 - CHUNKS_PAIRS
                signal = (acc_ready, done)
            if not last:
                used += 1
                signal = (w_used, used)
            chunk_used.append(signal)

        def taken(panel, t):
            return 8 + 8 * panel + t + 1

        def squares_of(n, t):
            return t + 1 if n == 0 else 16 * n + t + 1

        block = ctx.enter_context(nc.Block())

        @block.sync
        def _(sp):
            xt = x[0].rearrange("(t p) d -> t p d", p=P)
            sp.dma_start(c_raw[:], const[:, 0:C_EARLY]).then_inc(consts_loaded, 16)
            sp.dma_start(buf[0][:, 0, :], xt[0]).then_inc(tile_loaded[0], 16)
            sp.dma_start(lam_row[:, 0:4 * HEAD_DIM], lams).then_inc(lam_loaded, 16)
            sp.dma_start(g_rows[:], attn_norm_g[0:1, :].broadcast_to([P, D_MODEL])).then_inc(g_loaded, 16)
            for t in range(1, NT):
                sp.dma_start(buf[0][:, t, :], xt[t]).then_inc(tile_loaded[t], 16)
            sp.dma_start(gate_raw[:, :, 0:8], attn_w_in[0][:, COL_FF:COL_FF + 8].rearrange("(k p) c -> p k c", p=P)).then_inc(small_loaded, 16)
            sp.dma_start(gate_b[:, 0:1], fox_b_f.rearrange("a h -> h a")).then_inc(small_loaded, 16)
            sp.dma_start(gate_b[:, 1:3], ml_b).then_inc(small_loaded, 16)
            sp.dma_start(sub_g[:], subln_g[0:1, :].broadcast_to([P, P])).then_inc(small_loaded, 16)
            sp.dma_start(pos_i[:], positions[0:1, :].broadcast_to([P, SEQ])).then_inc(pos_loaded, 16)

            def chunk(n, src):
                if n + 1 - RING > 0:
                    sp.wait_ge(w_ready, n + 1 - RING)
                sp.dma_start(w_raw[:, n % RING, :], src).then_inc(raw_loaded[n % RING], 16)

            def load_panels(first, n, w, col, stride, lo=0):
                for i in range(lo, n * NK):
                    p, k = divmod(i, NK)
                    c = col + p * stride
                    chunk(first + i, w[k * P:(k + 1) * P, c:c + PANEL])

            def load_first(first, w, col):
                for k in range(RING):
                    chunk(first + k, w[k * P:(k + 1) * P, col:col + PANEL])

            load_panels(FIRST_V, 2, attn_w_in[0], COL_FV, COL_DV - COL_FV)
            for u in range(PAIRS):
                j = u // 2
                for i, c in enumerate((COL_DQ, COL_DK) if u % 2 else (COL_FQ, COL_FK)):
                    for g in range(2):
                        src = attn_w_in[0][g * 512:(g + 1) * 512, c + P * j:c + P * j + P]
                        n = FIRST_PAIRS + 4 * u + 2 * i + g
                        sp.wait_ge(w_ready, n + 1 - RING)
                        sp.dma_start(w_raw[:, n % RING, :].rearrange("p (k c) -> p k c", k=4),
                                     src.rearrange("(k p) c -> p k c", p=P)).then_inc(raw_loaded[n % RING], 16)
            load_first(FIRST_Z, attn_w_in[0], COL_AZ)
            load_panels(FIRST_Z, 2, attn_w_in[0], COL_AZ, PANEL, RING)
            sp.wait_ge(pv_free, 8 * PAIRS)
            for t in range(NT):
                sp.dma_start(buf[1][:, t, :], xt[t]).then_inc(x_again[t], 16)
            load_panels(FIRST_O0, 2, attn_w_out[0], 0, PANEL)
            sp.dma_start(g_rows[:], ml_norm_g[0:1, :].broadcast_to([P, D_MODEL])).then_inc(g1_loaded, 16)
            sp.wait_ge(gate_acc, 2)
            sp.dma_start(gate_raw[:], ml_w_in[0][:, COL_MG:COL_MG + 16].rearrange("(k p) c -> p k c", p=P)).then_inc(g1_loaded, 16)
            load_first(FIRST_A, ml_w_in[0], COL_MQ)
            for t in range(NT):
                sp.wait_ge(bank_free, taken(5, t))
                sp.dma_start(x1_scr[t * P:(t + 1) * P, :], buf[1][:, t, :]).then_inc(x1_stored, 16)
            sp.wait_ge(turned, 48)
            sp.dma_start(reset[:], const[0:8, C_RESET:C_RESET + SEQ]).then_inc(ml_loaded, 16)
            sp.wait_ge(gate_in, 1)
            sp.dma_start(gr[0][:], g_in[8:16, :]).then_inc(gate_moved, 16)
            load_panels(FIRST_A, 4, ml_w_in[0], COL_MQ, PANEL, RING)
            def load_neg_m(c):
                sp.dma_start(decay[c % 3][:], m_scr[:, c * P:(c + 1) * P].unsqueeze(0).broadcast_to(
                    [P, ML_HEADS, P])).then_inc(m_loaded[c % 3], 16)
            sp.wait_ge(m_stored, 16)
            for c in range(3):
                load_neg_m(c)
            load_panels(FIRST_B, 4, ml_w_in[0], COL_MO, PANEL)
            load_first(FIRST_O1, ml_w_out[0], 0)
            for c in range(3, NT):
                sp.wait_ge(sd_ready, 2 * (c - 2))
                load_neg_m(c)
            sp.wait_ge(kw_ready, NT)
            sp.wait_ge(qd_ready, NT)
            sp.wait_ge(k_turned, NT)
            sp.wait_ge(x1_stored, 16 * NT)
            for t in range(NT):
                sp.dma_start(buf[0][:, t, :], x1_scr[t * P:(t + 1) * P, :]).then_inc(tile_loaded[t], 16)
            load_panels(FIRST_O1, 2, ml_w_out[0], 0, PANEL, RING)
            sp.wait_ge(turned, 64)
            sp.dma_start(g_rows[:], final_norm_g.rearrange("(a d) -> a d", a=1).broadcast_to([P, D_MODEL])).then_inc(g2_loaded, 16)
            ot = out[0].rearrange("(t p) d -> t p d", p=P)
            for t in range(NT):
                sp.wait_ge(xn_ready, 2 * NT + t + 1)
                sp.dma_start(ot[t], buf[1][:, t, :]).then_inc(out_stored, 16)
            sp.wait_ge(out_stored, 16 * NT)

        @block.tensor
        def _(pe):
            def turn_half(stage, n, src, t, m):
                if n >= 8:
                    pe.wait_ge(turned_lo, 16 * stage + n - 7)
                for k in range(4):
                    last = pe.transpose(bank[:, n % 8, k * P:(k + 1) * P],
                                        src[:, t, (4 * m + k) * P:(4 * m + k + 1) * P], ident[:])
                last.then_inc(turned, 1)

            def turn_tiles(stage, src, ready, base, panel=None):
                for t in range(NT):
                    if panel is not None and t < NT // 2:
                        pe.wait_ge(bank_free, taken(panel, 2 * t + 1))
                    pe.wait_ge(ready, base + t + 1)
                    for m in range(2):
                        turn_half(stage, 2 * t + m, src, t, m)

            def gates(stage, width):
                for n in range(2):
                    pe.wait_ge(turned_lo, 16 * stage + 8 * n + 8)
                    for k in range(NK):
                        for g, part in ((gate_hi, ht_hi), (gate_lo, ht_hi), (gate_hi, ht_lo)):
                            last = pe.matmul(bank[0:width, n, :], g[:, k, 0:width],
                                             part[:, k, n * PANEL:(n + 1) * PANEL],
                                             start=(k == 0 and g is gate_hi and part is ht_hi),
                                             stop=(k == NK - 1 and part is ht_lo))
                    last.then_inc(gate_acc, 1)

            def panel_products(first_panel, first_chunk, n):
                def body(p):
                    for k in range(NK):
                        slot = k % RING
                        pe.wait_ge(w_ready, p * NK + (first_chunk + k + 1))
                        for t in range(NT):
                            if k == 0:
                                pe.wait_ge(bank_free, p * 8 + (first_panel * 8 + t + 1))
                            acc = bank[:, t, :]
                            hi, lo = ht_hi[:, k, t * P:(t + 1) * P], ht_lo[:, k, t * P:(t + 1) * P]
                            pe.matmul(acc, hi, w_hi[:, slot, :], start=(k == 0), stop=False)
                            pe.matmul(acc, hi, w_lo[:, slot, :], start=False, stop=False)
                            last = pe.matmul(acc, lo, w_hi[:, slot, :], start=False, stop=(k == NK - 1))
                            if k == NK - 1 and t < NT - 1:
                                last.then_inc(acc_ready, 1)
                        last.then_inc(acc_ready if k == NK - 1 else w_used, 1)
                panels(pe, n, body)

            pe.sem_inc(bank_free, 8)
            pe.wait_ge(consts_ready, 1)
            turn_tiles(0, buf[1], xn_ready, 0)
            pe.wait_ge(gate_split, 1)
            gates(0, 8)
            pe.wait_ge(lam_one, 1)
            pe.wait_ge(turned_lo, 16)
            pe.matmul(bank[:, 2, 0:1], lam_row[:, 0:P], lam_row[:, 4 * HEAD_DIM + 5:4 * HEAD_DIM + 6],
                      start=True, stop=True).then_inc(lam_bc, 1)
            pe.wait_ge(gate_u, 1)
            pe.wait_ge(lam_ready, 1)
            panel_products(0, FIRST_V, 2)

            def proj_steps(u, lo, hi):
                for n in range(lo, hi):
                    g, r = n // 24, n % 24
                    k, part = r // 3, r % 3
                    half, i = g % 2, g // 2
                    slot = 2 * i + k // 4
                    first = FIRST_PAIRS + 4 * u
                    if r == 0:
                        before_u, before_g = divmod(4 * u + g - 2, 4)
                        if before_u >= 0 and before_u % 2:
                            pe.wait_ge(pj_free, 4 * (before_u // 2) + before_g + 1)
                        else:
                            if 4 * u + g - 1 > 0:
                                pe.wait_ge(qk_ready, 4 * u + g - 1)
                    if r % 12 == 0:
                        pe.wait_ge(w_ready, first + slot + 1)
                    w = (w_hi, w_hi, w_lo)[part][:, slot, (k % 4) * P:(k % 4 + 1) * P]
                    h = (ht_hi, ht_lo, ht_hi)[part][:, k, half * PANEL:(half + 1) * PANEL]
                    last = pe.matmul(bank[:, g % 2, :], w, h, start=(r == 0), stop=(r == 23))
                    if r == 23:
                        last.then_inc(proj_done, 1)
                    if half == 1 and r == 11:
                        last.then_inc(w_used, 1)

            def rotate(u, g):
                if u < PAIRS and u % 2:
                    pe.wait_ge(pj_copied, 4 * (u // 2) + g + 1)
                    pe.matmul(bank[:, g % 2, :], perm[:], qs[:], start=True, stop=True).then_inc(perm_done, 1)

            pe.wait_ge(bank_free, taken(1, 7))
            proj_steps(0, 0, 96)

            for u in range(PAIRS):
                kind, nxt = u % 2, u + 1
                fill = [0]

                def filler(n):
                    if nxt < PAIRS:
                        proj_steps(nxt, fill[0], fill[0] + n)
                        fill[0] += n

                rows_max, rows_exp, m_w = (66, 68, 4) if kind == 0 else (64, 66, 2)
                QA, QB, KA, KB = q_a[kind], q_b[kind], k_a[kind], k_b[kind]

                def max_products(a, lo, hi, fill_n):
                    for n in range(lo, hi):
                        i, k0, w = MAX_CHUNKS[n]
                        if 24 * u + 12 * a + n - 1 > 0:
                            pe.wait_ge(max_done, 24 * u + 12 * a + n - 1)
                        acc = bank[:, 2 + n % 2, :]
                        qt, kt = slice(i * P, (i + 1) * P), slice(k0 * P, (k0 + w) * P)
                        diag = i < k0 + w
                        pe.matmul(acc[:, 0:w * P], QA[a][:, qt], KA[a][:, kt], start=True, stop=False)
                        last = pe.matmul(acc[:, 0:w * P], QB[a][0:rows_max, qt], KB[a][0:rows_max, kt],
                                         start=False, stop=not diag)
                        if diag:
                            last = pe.matmul(acc[:, (i - k0) * P:(i - k0 + 1) * P], ident_r[:], mask_q[:],
                                             start=False, stop=True)
                        last.then_inc(max_in, 1)
                        filler(fill_n)

                def turn_maximum(a):
                    pe.wait_ge(m_ready, 2 * u + a + 1)
                    pe.wait_ge(max_done, 24 * u + 24)
                    if a == 1:
                        pe.wait_ge(m_rows, 4 * u + 2)
                    for half in range(2):
                        for t in range(4):
                            last = pe.transpose(bank[0:m_w, 2 + half, t * P:(t + 1) * P],
                                                m_cols[:, a, 4 * half + t, 4 - m_w:4].bitcast(F32), ident[:])
                        last.then_inc(m_turned, 1)

                def exp_products(a, lo, hi, fill_n):
                    for n in range(lo, hi):
                        if n % 4 == 0 and n < 8:
                            pe.wait_ge(m_rows, 4 * u + 2 * a + n // 4 + 1)
                        k, t0, t1 = EXP_CHUNKS[n]
                        if 24 * u + 12 * a + n - 1 > 0:
                            pe.wait_ge(probs_ready, 24 * u + 12 * a + n - 1)
                        acc = bank[:, 4 + n % 2, :]
                        kt, qt = slice(k * P, (k + 1) * P), slice(t0 * P, t1 * P)
                        w = (t1 - t0) * P
                        pe.matmul(acc[:, 0:w], KA[a][:, kt], QA[a][:, qt], start=True, stop=False)
                        last = pe.matmul(acc[:, 0:w], KB[a][0:rows_exp, kt], QB[a][0:rows_exp, qt],
                                         start=False, stop=k != t0)
                        if k == t0:
                            last = pe.matmul(acc[:, 0:P], ident_r[:], mask_k[:], start=False, stop=True)
                        last.then_inc(exp_in, 1)
                        filler(fill_n)

                def value_products(a, lo, hi):
                    width = 65 if kind == 0 else 129
                    v0 = 65 * a if kind == 0 else 0
                    for b in range(lo, hi):
                        pe.wait_ge(probs_ready, 24 * u + 12 * a + (4 if b < 2 else 12))
                        if 8 * u + 4 * a + b - 1 > 0:
                            pe.wait_ge(pv_free, 8 * u + 4 * a + b - 1)
                        for i in (2 * b, 2 * b + 1):
                            for k in range(i + 1):
                                at = EXP_AT[(k, i // 4)] + i * P
                                last = pe.matmul(bank[:, 6 + b % 2, (i % 2) * width:(i % 2 + 1) * width],
                                                 probs[:, at:at + P], v_pair[kind][:, k, v0:v0 + width],
                                                 start=(k == 0), stop=(k == i))
                        last.then_inc(pv_ready, 1)

                pe.wait_ge(qk_ready, 4 * u + 4)
                pe.wait_ge(qk_twice, 8 * (u + 1))
                if kind == 0:
                    pe.wait_ge(rowf_loaded, 32 * (u // 2 + 1))
                max_products(0, 0, 12, 2)
                max_products(1, 0, 5, 2)
                rotate(nxt, 0)
                max_products(1, 5, 12, 2)
                filler(2)
                turn_maximum(0)
                filler(4)
                exp_products(0, 0, 3, 2)
                turn_maximum(1)
                exp_products(0, 3, 5, 2)
                rotate(nxt, 1)
                exp_products(0, 5, 6, 2)
                exp_products(0, 6, 12, 4)
                rotate(nxt, 2)
                pe.wait_ge(v_loaded[kind], 32 // (1 + kind) * (u // 2 + 1))
                value_products(0, 0, 2)
                exp_products(1, 0, 3, 2)
                exp_products(1, 3, 4, 0)
                value_products(0, 2, 4)
                exp_products(1, 4, 8, 0)
                rotate(nxt, 3)
                exp_products(1, 8, 12, 0)
                value_products(1, 0, 4)

            pe.wait_ge(pv_free, 8 * PAIRS)
            panel_products(2, FIRST_Z, 2)
            for m in range(2):
                for t in range(NT):
                    pe.wait_ge(bank_free, taken(3, t))
                    pe.wait_ge(y_ready, 8 * m + t + 1)
                    turn_half(1, 8 * m + t, buf[0], t, m)
            pe.wait_ge(turned_lo, 32)
            panel_products(4, FIRST_O0, 2)
            turn_tiles(2, buf[0], xn_ready, NT, 5)
            pe.wait_ge(gate_split, 2)
            gates(2, 16)
            pe.wait_ge(gate_in, 1)
            panel_products(6, FIRST_A, 4)
            pe.wait_ge(bank_free, taken(9, 7))
            pe.wait_ge(gate_l, 1)
            for c in range(NT):
                last = pe.transpose(bank[:, c // 4, (c % 4) * 104:(c % 4) * 104 + 104],
                                    rows4[0:104, c * P:(c + 1) * P], ident[0:104, 0:104])
                if c % 4 == 3:
                    last.then_inc(cols_turned, 1)
            pe.matmul(bank[:, 2, 0:NT * ML_HEADS], ones8[:], lrow[:, :, 0:8], start=True,
                      stop=True).then_inc(wold_bc, 1)
            pe.wait_ge(cols_ready, 3)
            panel_products(10, FIRST_B, 4)
            pe.wait_ge(bank_free, taken(13, 7))

            def turn_rows(to, src):
                for m in range(4):
                    last = pe.transpose(bank[:, to, m * P:(m + 1) * P], src[:, m * P:(m + 1) * P], ident[:])
                return last

            def turn_qk(c):
                if c > 0:
                    pe.wait_ge(qd_copied, c)
                    pe.wait_ge(k_ready, c)
                turn_rows(0, qk_rows[:, c, 0:PANEL]).then_inc(q_turned, 1)
                turn_rows(1, qk_rows[:, c, PANEL:2 * PANEL]).then_inc(k_turned, 1)

            def turn_decayed(c):
                pe.wait_ge(q_ready, c + 1)
                pe.wait_ge(qd_ready, c + 1)
                turn_rows(0, q_decayed[:].rearrange("p h d -> p (h d)")).then_inc(qd_turned, 1)

            def cell_scores(c):
                pe.wait_ge(q_ready, c + 1)
                pe.wait_ge(k_ready, c + 1)
                for r in range(2):
                    if c > 0:
                        pe.wait_ge(sd_ready, 2 * (c - 1) + r + 1)
                    rows = slice(64 * r, 64 * r + 64)
                    for m in range(4):
                        last = pe.matmul(bank[:, 2 + r, m * P:(m + 1) * P], k_t[c % 2][rows, m, :],
                                         q_t[c % 2][rows, m, :], start=True, stop=True)
                    last.then_inc(s_in, 1)

            def cell_outputs(c, mm):
                banks = [4 + 2 * mm, 5 + 2 * mm]
                if c > 0:
                    pe.wait_ge(state_ready, 2 * (c - 1) + mm + 1)
                pe.wait_ge(sd_ready, 2 * c + 2)
                pe.wait_ge(qd_copied, c + 1)
                pe.wait_ge(kw_ready, c + 1)
                for i in range(2):
                    m = 2 * mm + i
                    for r in range(2):
                        pe.matmul(bank[:, banks[r], i * 129:(i + 1) * 129], sd[2 * (c % 2) + r][:, m, :],
                                  v_rows[:, c, 2 * m + r, 0:129], start=True, stop=False)
                    for r in range(2):
                        pe.matmul(bank[:, banks[r], i * 129:(i + 1) * 129],
                                  qd_t[c % 2][64 * r:64 * r + 64, m, :],
                                  state[64 * r:64 * r + 64, m, 0:129], start=False, stop=True)
                for i in range(2):
                    m = 2 * mm + i
                    for r in range(2):
                        last = pe.matmul(bank[64 * r:64 * r + 64, banks[i], 258:387],
                                         kw[c % 2][:, 2 * m + r, :], v_rows[:, c, 2 * m + r, 0:129],
                                         start=True, stop=True)
                last.then_inc(inter_in, 1)

            turn_qk(0)
            cell_scores(0)
            turn_decayed(0)
            pe.wait_ge(ml_init, 1)
            for c in range(NT):
                if c + 1 < NT:
                    turn_qk(c + 1)
                cell_outputs(c, 0)
                if c + 1 < NT:
                    cell_scores(c + 1)
                    turn_decayed(c + 1)
                cell_outputs(c, 1)
            pe.wait_ge(state_ready, 2 * NT)
            for t in range(NT):
                pe.wait_ge(state_ready, 2 * (t + 1))
                for m in range(2):
                    turn_half(3, 2 * t + m, gl_rows, t, m)
            pe.wait_ge(turned_lo, 64)
            panel_products(14, FIRST_O1, 2)

        @block.scalar
        def _(act):
            def split_hi(lo, hi):
                for n in range(lo, hi):
                    act.wait_ge(raw_loaded[n % RING], 16 * (n // RING + 1))
                    if n >= RING:
                        producer, count = chunk_used[n - RING]
                        act.wait_ge(producer, count)
                    act.activation(w_hi[:, n % RING, :], w_raw[:, n % RING, :], ACT.Copy).then_inc(hi_split, 1)

            def turn_hi(stage, n, t, m):
                act.wait_ge(turned, 16 * stage + n + 1)
                act.activation(ht_hi[:, 4 * m:4 * m + 4, t * P:(t + 1) * P],
                               bank[:, n % 8, :].rearrange("p (k c) -> p k c", k=4),
                               ACT.Copy).then_inc(turned_hi, 1)

            def squares(src, junk, t, part, cols):
                act.activation(junk[:, t, cols], src[:, t, cols], ACT.Square,
                               accum_out=stat[:, part, t:t + 1]).then_inc(squares_ready, 1)

            def half_squares(first_panel, src, junk, p, t):
                act.wait_ge(bank_free, taken(first_panel + p, t))
                squares(src, junk, t, 3 * p, slice(p * PANEL, (p + 1) * PANEL))

            def panel_stage(first_panel, first_chunk, n, take=None, split=3):
                for p in range(n):
                    c = first_chunk + NK * p
                    split_hi(c + (split if p == 0 else 3), c + NK)
                    if p + 1 < n:
                        split_hi(c + NK, c + NK + 3)
                    for t in range(NT if take else 0):
                        act.wait_ge(acc_ready, 8 * (first_panel + p) + t + 1)
                        take(p, t)

            act.wait_ge(lam_sum, 1)
            act.activation(lam_row[:, 258:260], lam_row[:, 256:258], ACT.Exp).then_inc(lam_exp, 1)
            for t in range(NT + 2):
                if t < NT:
                    act.wait_ge(tile_loaded[t], 16)
                    squares(buf[0], buf[1], t, 0, slice(0, D_MODEL))
                if t >= 2:
                    for m in range(2):
                        turn_hi(0, 2 * (t - 2) + m, t - 2, m)
            split_hi(FIRST_V, FIRST_V + 3)
            act.wait_ge(gate_e, 1)
            act.activation(row[1][:], row[1][:], ACT.Exp, scale=-1.0).then_inc(gate_exp, 1)
            act.wait_ge(gate_exp, 1)
            act.activation(row[1][:], row[1][:], ACT.Ln, bias=1.0).then_inc(gate_ln, 1)

            def take_v(p, t):
                if 16 * p > 0:
                    act.wait_ge(v_stored[t], 16 * p)
                act.activation(v_stage[:, t, :], bank[:, t, :],
                               ACT.Copy).then_inc(bank_free, 1)
            split_hi(FIRST_V + 3, FIRST_V + 5)
            act.wait_ge(rope_args, 1)
            act.activation(sin_t[:], angle[:], ACT.Sin)
            act.activation(cos_t[:], turn[:], ACT.Sin).then_inc(rope_ready, 1)
            panel_stage(0, FIRST_V, 2, take_v, split=5)
            split_hi(FIRST_PAIRS, FIRST_PAIRS + 4)

            def copy_rotary(u, g):
                act.wait_ge(proj_done, 4 * u + g + 1)
                if 4 * (u // 2) + g > 0:
                    act.wait_ge(roped, 4 * (u // 2) + g)
                act.activation(qs[:], bank[:, g % 2, :], ACT.Copy).then_inc(pj_copied, 1)

            def round_group(u, g):
                kind, half = u % 2, slice((g % 2) * PANEL, (g % 2 + 1) * PANEL)
                if kind:
                    act.wait_ge(roped, 4 * (u // 2) + g + 1)
                else:
                    act.wait_ge(proj_done, 4 * u + g + 1)
                for a in range(2):
                    r = slice(64 * a, 64 * a + 64)
                    src = rot[r, :] if kind else bank[r, g % 2, :]
                    act.activation((q_a if g < 2 else k_a)[kind][a][r, half], src,
                                   ACT.Copy).then_inc(qk_hi, 1)

            def head_squares(u):
                act.wait_ge(pv_free, 8 * (u + 1))
                for i in range(NT):
                    act.activation(sub_sq[:, i, :], o_pair[1][:, i, :], ACT.Square,
                                   accum_out=sub_ss[:, 0, i:i + 1]).then_inc(o_squares, 1)

            for t in range(NT):
                act.wait_ge(v_stored[t], 32)
            act.wait_ge(helper_init, 1)
            for g in range(4):
                round_group(0, g)

            for u in range(PAIRS):
                nxt = u + 1
                more, after = nxt < PAIRS, u + 2 < PAIRS
                rotary = nxt % 2 == 1

                def exps(a, lo, hi):
                    for n in range(lo, hi):
                        k, t0, t1 = EXP_CHUNKS[n]
                        if n == 0:
                            if 8 * u + 4 * a - 2 > 0:
                                act.wait_ge(pv_ready, 8 * u + 4 * a - 2)
                        if n == 4:
                            if 8 * u + 4 * a > 0:
                                act.wait_ge(pv_ready, 8 * u + 4 * a)
                        act.wait_ge(exp_in, 24 * u + 12 * a + n + 1)
                        at = EXP_AT[(k, n // 4 and 1)] + t0 * P
                        act.activation(probs[:, at:at + (t1 - t0) * P], bank[:, 4 + n % 2, 0:(t1 - t0) * P],
                                       ACT.Exp, scale=HEAD_DIM ** -0.5).then_inc(probs_ready, 1)

                if u == 0:
                    split_hi(FIRST_PAIRS + 4, FIRST_PAIRS + 6)
                if more:
                    split_hi(FIRST_PAIRS + 4 * nxt + 2, FIRST_PAIRS + 4 * nxt + 4)
                if u and u % 2 == 0:
                    head_squares(u - 1)
                if more and rotary:
                    copy_rotary(nxt, 0)
                    exps(0, 0, 2)
                    round_group(nxt, 0)
                    copy_rotary(nxt, 1)
                    exps(0, 2, 8)
                    round_group(nxt, 1)
                    exps(0, 8, 11)
                    copy_rotary(nxt, 2)
                    exps(0, 11, 12)
                elif more:
                    round_group(nxt, 0)
                    round_group(nxt, 1)
                    exps(0, 0, 8)
                    round_group(nxt, 2)
                    exps(0, 8, 12)
                else:
                    exps(0, 0, 12)
                if after:
                    split_hi(FIRST_PAIRS + 4 * (u + 2), FIRST_PAIRS + 4 * (u + 2) + 2)
                if u == PAIRS - 1:
                    split_hi(FIRST_Z, FIRST_Z + 3)
                exps(1, 0, 4)
                if more and rotary:
                    round_group(nxt, 2)
                    copy_rotary(nxt, 3)
                exps(1, 4, 10)
                if more:
                    round_group(nxt, 3)
                exps(1, 10, 12)

            head_squares(PAIRS - 1)

            def take_z(p, t):
                n = p * 8 + t
                if n - 1 > 0:
                    act.wait_ge(y_ready, n - 1)
                act.activation(silu[:, n % 2, :], bank[:, t, :],
                               ACT.Silu).then_inc(bank_free, 1)
            panel_stage(2, FIRST_Z, 2, take_z)
            split_hi(FIRST_O0, FIRST_O0 + 3)
            for m in range(2):
                for t in range(NT):
                    turn_hi(1, 8 * m + t, t, m)

            def residual_squares(first_panel, first_chunk, src, junk):
                split_hi(first_chunk + 3, first_chunk + NK + 3)
                for t in range(NT):
                    half_squares(first_panel, src, junk, 0, t)
                split_hi(first_chunk + NK + 3, first_chunk + 2 * NK)
            residual_squares(4, FIRST_O0, buf[1], buf[0])
            for t in range(NT + 4):
                if t < NT:
                    half_squares(4, buf[1], buf[0], 1, t)
                if t >= 4:
                    for m in range(2):
                        turn_hi(2, 2 * (t - 4) + m, t - 4, m)
            split_hi(FIRST_A, FIRST_A + 3)
            act.wait_ge(gate_e, 2)
            act.activation(gr[1][:], gr[1][:], ACT.Exp, scale=-1.0).then_inc(gate_exp, 1)
            act.wait_ge(gate_exp, 2)
            act.activation(gr[1][:], gr[1][:], ACT.Ln, bias=1.0).then_inc(gate_ln, 1)

            def take_a(p, t):
                if p < 2:
                    dst = qk_rows[:, t, p * PANEL:(p + 1) * PANEL]
                    src = bank[:, t, :]
                else:
                    dst = v_rows[:, t, 4 * (p - 2):4 * (p - 1), 0:P]
                    src = bank[:, t, :].rearrange("p (h e) -> p h e", h=4)
                act.activation(dst, src, ACT.Copy).then_inc(bank_free, 1)
            act.wait_ge(x1_stored, 16 * NT)
            panel_stage(6, FIRST_A, 4, take_a)

            def take_b(p, t):
                if p < 2:
                    act.activation(gl_rows[:, t, p * PANEL:(p + 1) * PANEL], bank[:, t, :],
                                   ACT.Sigmoid).then_inc(bank_free, 1)
                else:
                    n = (p - 2) * 8 + t
                    if n - 1 > 0:
                        act.wait_ge(gl_ready, n - 1)
                    act.activation(zs[:, n % 2, :], bank[:, t, :],
                                   ACT.Silu).then_inc(bank_free, 1)
            split_hi(FIRST_B, FIRST_B + 3)
            for b in range(2):
                act.wait_ge(cols_turned, b + 1)
                src = bank[:, b, 0:416].rearrange("p (c k e) -> p c k e", c=4, k=13)
                act.activation(cols[:, 4 * b:4 * b + 4, 0, :], src[:, :, 0, :], ACT.Copy)
                for kind in range(1, 4):
                    last = act.activation(cols[:, 4 * b:4 * b + 4, kind, :], src[:, :, 4 * kind, :], ACT.Exp)
                last.then_inc(cols_ready, 1)
            act.wait_ge(wold_bc, 1)
            src = bank[:, 2, 0:NT * ML_HEADS].rearrange("p (c m r) -> p c m r", c=NT, r=2)
            act.activation(w_old[0:64, :, 0:4], src[0:64, :, :, 0], ACT.Exp)
            act.activation(w_old[64:128, :, 0:4], src[64:128, :, :, 1], ACT.Exp).then_inc(cols_ready, 1)

            def cell_decay(c):
                act.wait_ge(mask_ready, c + 1)
                for h in range(ML_HEADS):
                    d = decay[c % 3][:, h, :]
                    last = act.activation(d, d, ACT.Exp, bias=cols[:, c, 0, h:h + 1])
                last.then_inc(d_ready, 1)
            split_hi(FIRST_B + 3, FIRST_B + 4)
            cell_decay(0)
            cell_decay(1)
            act.wait_ge(m_stored, 16)
            panel_stage(10, FIRST_B, 4, take_b, split=4)
            split_hi(FIRST_O1, FIRST_O1 + 3)

            def cell_q(c):
                act.wait_ge(q_turned, c + 1)
                if c > 1:
                    act.wait_ge(s_in, 2 * (c - 1))
                act.activation(q_t[c % 2][:], bank[:, 0, :].rearrange("p (m c) -> p m c", m=4), ACT.Copy,
                               scale=ML_QK ** -0.5).then_inc(q_ready, 1)
                act.wait_ge(k_turned, c + 1)
                act.activation(k_t[c % 2][:], bank[:, 1, :].rearrange("p (m c) -> p m c", m=4),
                               ACT.Copy).then_inc(k_ready, 1)

            def cell_decayed(c):
                act.wait_ge(qd_turned, c + 1)
                if c > 1:
                    act.wait_ge(inter_in, 2 * (c - 1))
                act.activation(qd_t[c % 2][:], bank[:, 0, :].rearrange("p (m c) -> p m c", m=4), ACT.Copy,
                               scale=ML_QK ** -0.5).then_inc(qd_copied, 1)

            cell_q(0)
            cell_decayed(0)
            for c in range(NT):
                if c + 1 < NT:
                    cell_q(c + 1)
                if c + 2 < NT:
                    cell_decay(c + 2)
                if c + 1 < NT:
                    cell_decayed(c + 1)
            act.wait_ge(state_ready, 2 * NT)
            for t in range(NT):
                for m in range(2):
                    turn_hi(3, 2 * t + m, t, m)
            residual_squares(14, FIRST_O1, buf[0], buf[1])
            for t in range(NT):
                half_squares(14, buf[0], buf[1], 1, t)

        @block.vector
        def _(dve):
            steps = [0]

            def step(ins):
                steps[0] += 1
                ins.then_inc(dve_chain, 1)
                dve.wait_ge(dve_chain, steps[0])

            V = nc.vector

            def split_lo(lo, hi):
                for n in range(lo, hi):
                    dve.wait_ge(hi_split, n + 1)
                    V.tensor_tensor(w_lo[:, n % RING, :], w_raw[:, n % RING, :],
                                    w_hi[:, n % RING, :].bitcast(F32), ALU.subtract).then_inc(w_ready, 1)

            def turn_lo(stage, n, t, m):
                dve.wait_ge(turned_hi, 16 * stage + n + 1)
                V.tensor_tensor(ht_lo[:, 4 * m:4 * m + 4, t * P:(t + 1) * P],
                                bank[:, n % 8, :].rearrange("p (k c) -> p k c", k=4),
                                ht_hi[:, 4 * m:4 * m + 4, t * P:(t + 1) * P].bitcast(F32),
                                ALU.subtract).then_inc(turned_lo, 1)

            def normalise(n, src, dst, t):
                dve.wait_ge(rstd_ready, NT * n + t + 1)
                V.scalar_tensor_tensor(out=dst[:, t, :], in0=src[:, t, :], scalar=stat[:, 2, t:t + 1],
                                       in1=g_rows[:], op0=ALU.mult, op1=ALU.mult).then_inc(xn_ready, 1)

            def split_gates(w):
                step(V.tensor_copy(gate_hi[:, :, 0:w], gate_raw[:, :, 0:w]))
                V.tensor_tensor(gate_lo[:, :, 0:w], gate_raw[:, :, 0:w], gate_hi[:, :, 0:w].bitcast(F32),
                                ALU.subtract).then_inc(gate_split, 1)

            def panel_stage(first_panel, first_chunk, n, take=None, split=3):
                for p in range(n):
                    c = first_chunk + NK * p
                    split_lo(c + (split if p == 0 else 3), c + NK)
                    if p + 1 < n:
                        split_lo(c + NK, c + NK + 3)
                    for t in range(NT if take else 0):
                        dve.wait_ge(acc_ready, 8 * (first_panel + p) + t + 1)
                        take(p, t)

            def log_gate(u, a, src, bias, n):
                V.tensor_scalar(u, src, bias, None, ALU.add).then_inc(gate_u, 1)
                dve.wait_ge(gate_u, n)
                V.scalar_tensor_tensor(out=a, in0=u, scalar=-1.0, in1=u, op0=ALU.mult,
                                       op1=ALU.max).then_inc(gate_e, 1)
                dve.wait_ge(gate_ln, n)
                step(V.scalar_tensor_tensor(out=u, in0=u, scalar=0.0, in1=a, op0=ALU.min, op1=ALU.subtract))

            dve.wait_ge(consts_loaded, 16)
            for dst, c in ((ident, C_IDENT), (perm, C_PERM), (ident_r, C_IDENT),
                           (mask_q, C_MASKQ), (mask_k, C_MASKK)):
                V.tensor_copy(dst[:], c_raw[:, c:c + P])
            V.tensor_copy(inv_sign[:], c_raw[:, C_INV:C_INV + 2]).then_inc(consts_ready, 1)
            dve.wait_ge(consts_ready, 1)
            dve.wait_ge(lam_loaded, 16)
            pairs_l = lam_row[:, 0:4 * HEAD_DIM].rearrange("p (a b c) -> p a b c", a=2, b=2)
            step(V.tensor_tensor(pairs_l[:, :, 0, :], pairs_l[:, :, 0, :], pairs_l[:, :, 1, :], ALU.mult))
            V.tensor_reduce(lam_row[:, 256:258], pairs_l[:, :, 0, :], AX.X, ALU.add).then_inc(lam_sum, 1)
            dve.wait_ge(lam_sum, 1)
            dve.wait_ge(lam_exp, 1)
            step(V.tensor_tensor(lam_row[:, 260:261], lam_row[:, 258:259], lam_row[:, 259:260], ALU.subtract))
            step(V.tensor_scalar(lam_row[:, 261:262], lam_row[:, 260:261], -1.0, -LAM_INIT, ALU.mult, ALU.add))
            V.memset(lam_row[:, 0:P], 1.0).then_inc(lam_one, 1)
            dve.wait_ge(g_loaded, 16)
            for t in range(NT + 2):
                if t < NT:
                    normalise(0, buf[0], buf[1], t)
                if t == 3:
                    dve.wait_ge(small_loaded, 64)
                    split_gates(8)
                if t >= 2:
                    for m in range(2):
                        turn_lo(0, 2 * (t - 2) + m, t - 2, m)
            split_lo(FIRST_V, FIRST_V + 3)
            dve.wait_ge(gate_acc, 2)
            log_gate(row[0][:].rearrange("p (a b) -> p a b", a=2), row[1][:].rearrange("p (a b) -> p a b", a=2),
                     bank[0:8, 0:2, :], gate_b[:, 0:1], 1)
            dve.wait_ge(lam_bc, 1)
            V.tensor_copy(neg_lam[:], bank[:, 2, 0:1]).then_inc(lam_ready, 1)
            step(V.memset(f_parts[:, 0, :].bitcast(F32), 1.0))
            step(V.tensor_tensor_scan(row[1][:], f_parts[:, 0, :].bitcast(F32), row[0][:], 0.0, ALU.mult, ALU.add))
            step(V.tensor_scalar(f_parts[:, 0, :], row[1][:], -8.0, None, ALU.mult))
            V.scalar_tensor_tensor(out=f_parts[:, 1, :], in0=row[1][:], scalar=-8.0,
                                   in1=f_parts[:, 0, :].bitcast(F32), op0=ALU.mult,
                                   op1=ALU.subtract).then_inc(f_ready, 1)
            split_lo(FIRST_V + 3, FIRST_V + 4)
            dve.wait_ge(pos_loaded, 16)
            step(V.tensor_copy(turn[:], pos_i[:]))
            step(V.tensor_scalar(angle[:], turn[:], inv_sign[:, 0:1], None, ALU.mult))
            step(V.tensor_scalar(turn[:], angle[:], 1.0 / (2.0 * math.pi), ROUND, ALU.mult, ALU.add))
            step(V.tensor_scalar(turn[:], turn[:], ROUND, None, ALU.subtract))
            for part in (TWO_PI_1, TWO_PI_2, TWO_PI_3):
                step(V.scalar_tensor_tensor(out=angle[:], in0=turn[:], scalar=-part, in1=angle[:],
                                            op0=ALU.mult, op1=ALU.add))
            step(V.tensor_scalar(angle[:], angle[:], PI_SAFE, -PI_SAFE, ALU.min, ALU.max))
            step(V.scalar_tensor_tensor(out=turn[:], in0=angle[:], scalar=-1.0, in1=angle[:],
                                        op0=ALU.mult, op1=ALU.max))
            V.tensor_scalar(turn[:], turn[:], -1.0, math.pi / 2, ALU.mult,
                            ALU.add).then_inc(rope_args, 1)
            split_lo(FIRST_V + 4, FIRST_V + 5)
            dve.wait_ge(turned, 16)
            for c in range(2):
                for a in range(2):
                    V.memset(q_b[c][a][64:68, :].bitcast(F32), 1.0)
                    V.memset(k_b[c][a][64:68, :].bitcast(F32), 1.0)
                V.memset(v_pair[c][:], 1.0)
            V.memset(m_cols[:].bitcast(F32), 1.0).then_inc(helper_init, 1)
            V.tensor_scalar(sub_g[:], sub_g[:], 1.0 - LAM_INIT, None, ALU.mult).then_inc(helper_sub, 1)
            dve.wait_ge(rope_ready, 1)
            step(V.tensor_scalar(sin_t[:], sin_t[:], inv_sign[:, 1:2], None, ALU.mult))
            panel_stage(0, FIRST_V, 2, split=5)
            split_lo(FIRST_PAIRS, FIRST_PAIRS + 4)

            def lo_group(u, g):
                kind, half = u % 2, slice((g % 2) * PANEL, (g % 2 + 1) * PANEL)
                dve.wait_ge(qk_hi, 2 * (4 * u + g + 1))
                for a in range(2):
                    r, other = slice(64 * a, 64 * a + 64), slice(64 - 64 * a, 128 - 64 * a)
                    src = rot[r, :] if kind else bank[r, g % 2, :]
                    if g < 2:
                        hi, dst = q_a[kind][a][r, half], q_b[kind][a][0:64, half]
                    else:
                        hi, dst = k_a[kind][a][r, half], k_a[kind][a][other, half]
                    last = V.tensor_tensor(dst, src, hi.bitcast(F32), ALU.subtract)
                last.then_inc(qk_ready, 1)

            def rope_cos(u, g):
                dve.wait_ge(pj_copied, 4 * (u // 2) + g + 1)
                dve.wait_ge(qk_ready, 4 * u + g)
                half = slice((g % 2) * PANEL, (g % 2 + 1) * PANEL)
                step(V.tensor_tensor(rot[:], qs[:], cos_t[:, half], ALU.mult))

            def rope_sin(u, g):
                dve.wait_ge(perm_done, 4 * (u // 2) + g + 1)
                half = slice((g % 2) * PANEL, (g % 2 + 1) * PANEL)
                V.tensor_tensor(qs[:], bank[:, g % 2, :], sin_t[:, half], ALU.mult).then_inc(pj_free, 1)
                dve.wait_ge(pj_free, 4 * (u // 2) + g + 1)
                V.tensor_tensor(rot[:], rot[:], qs[:], ALU.add).then_inc(roped, 1)

            for t in range(NT):
                dve.wait_ge(v_stored[t], 32)
            for g in range(4):
                lo_group(0, g)

            for u in range(PAIRS):
                kind, nxt = u % 2, u + 1
                more, after = nxt < PAIRS, u + 2 < PAIRS
                turn_n = nxt % 2 == 1

                def maxima(a, lo, hi):
                    for n in range(lo, hi):
                        w = MAX_CHUNKS[n][2]
                        dve.wait_ge(max_in, 24 * u + 12 * a + n + 1)
                        V.tensor_reduce(m_part[:, a, n:n + 1], bank[:, 2 + n % 2, 0:w * P], AX.X,
                                        ALU.max).then_inc(max_done, 1)

                def negate_maximum(a):
                    dve.wait_ge(max_done, 24 * u + 12 * a + 12)
                    step(V.tensor_copy(m_max[:, a, 0:4], m_part[:, a, 0:4]))
                    step(V.tensor_tensor(m_max[:, a, 4:8], m_part[:, a, 4:12:2], m_part[:, a, 5:12:2], ALU.max))
                    step(V.tensor_scalar(m_cols[:, a, :, 2], m_max[:, a, :], -1.0, None, ALU.mult))
                    V.scalar_tensor_tensor(out=m_cols[:, a, :, 3], in0=m_max[:, a, :], scalar=-1.0,
                                           in1=m_cols[:, a, :, 2].bitcast(F32), op0=ALU.mult,
                                           op1=ALU.subtract).then_inc(m_ready, 1)

                def maximum_rows(a):
                    w = 4 if kind == 0 else 2
                    for half in range(2):
                        dve.wait_ge(m_turned, 4 * u + 2 * a + half + 1)
                        V.tensor_copy(q_b[kind][a][64:64 + w, half * PANEL:(half + 1) * PANEL],
                                      bank[0:w, 2 + half, :]).then_inc(m_rows, 1)

                def outputs(a, lo, hi):
                    width = 65 if kind == 0 else 129
                    for b in range(lo, hi):
                        dve.wait_ge(pv_ready, 8 * u + 4 * a + b + 1)
                        at = slice(8 * a + 2 * b, 8 * a + 2 * b + 2)
                        pv = bank[:, 6 + b % 2, 0:2 * width].rearrange("p (i e) -> p i e", i=2)
                        values = pv[:, :, 0:width - 1]
                        tiles = slice(2 * b, 2 * b + 2)
                        step(V.reciprocal(recip[:, 0, at], pv[:, :, width - 1]))
                        if a == 1 and kind == 1:
                            step(V.tensor_scalar(recip[:, 1, at], recip[:, 0, at], neg_lam[:, 0:1], None, ALU.mult))
                            for i in range(2):
                                n, m = 2 * b + i, 8 * a + 2 * b + i
                                last = V.scalar_tensor_tensor(out=o_pair[1][:, n, :], in0=values[:, i, :],
                                                              scalar=recip[:, 1, m:m + 1],
                                                              in1=o_pair[1][:, n, :], op0=ALU.mult, op1=ALU.add)
                        else:
                            dst = o_pair[kind][:, tiles, 64 * a:64 * a + 64] if kind == 0 else o_pair[1][:, tiles, :]
                            last = V.tensor_tensor(dst, values, recip[:, 0, at].unsqueeze(2).broadcast_to(
                                [P, 2, width - 1]), ALU.mult)
                        last.then_inc(pv_free, 1)

                if u == 0:
                    split_lo(FIRST_PAIRS + 4, FIRST_PAIRS + 6)
                maxima(0, 0, 6)
                if more:
                    split_lo(FIRST_PAIRS + 4 * nxt + 2, FIRST_PAIRS + 4 * nxt + 4)
                maxima(0, 6, 12)
                negate_maximum(0)
                maxima(1, 0, 4)
                if more and turn_n:
                    rope_cos(nxt, 0)
                elif more:
                    lo_group(nxt, 0)
                maxima(1, 4, 9)
                if more and turn_n:
                    rope_sin(nxt, 0)
                maxima(1, 9, 12)
                negate_maximum(1)
                maximum_rows(0)
                maximum_rows(1)
                if more and turn_n:
                    lo_group(nxt, 0)
                    rope_cos(nxt, 1)
                    rope_sin(nxt, 1)
                if more:
                    lo_group(nxt, 1)
                if 16 * (u // 2) > 0:
                    dve.wait_ge(o_stored[kind], 16 * (u // 2))
                if u > 0:
                    dve.wait_ge(pv_free, 8 * u)
                if more and turn_n:
                    rope_cos(nxt, 2)
                outputs(0, 0, 2)
                if more and turn_n:
                    rope_sin(nxt, 2)
                if more:
                    lo_group(nxt, 2)
                outputs(0, 2, 4)
                if after:
                    split_lo(FIRST_PAIRS + 4 * (u + 2), FIRST_PAIRS + 4 * (u + 2) + 2)
                if u == PAIRS - 1:
                    split_lo(FIRST_Z, FIRST_Z + 3)
                if more and turn_n:
                    rope_cos(nxt, 3)
                    rope_sin(nxt, 3)
                if more:
                    lo_group(nxt, 3)
                outputs(1, 0, 4)

            def gate_outputs(p, t):
                dve.wait_ge(o_loaded[t], 16)
                dve.wait_ge(bank_free, taken(2 + p, t))
                d = buf[0][:, t, p * PANEL:(p + 1) * PANEL]
                V.tensor_tensor(d, d, silu[:, t % 2, :], ALU.mult).then_inc(y_ready, 1)
            panel_stage(2, FIRST_Z, 2, gate_outputs)
            split_lo(FIRST_O0, FIRST_O0 + 3)
            for m in range(2):
                for t in range(NT):
                    turn_lo(1, 8 * m + t, t, m)

            def residual(dst, arrived, count, first_panel, p, t):
                dve.wait_ge(arrived[t], count)
                dve.wait_ge(acc_ready, 8 * (first_panel + p) + t + 1)
                d = dst[:, t, p * PANEL:(p + 1) * PANEL]
                V.tensor_tensor(d, bank[:, t, :], d, ALU.add).then_inc(bank_free, 1)

            def first_residual(dst, arrived, count, first_panel, first_chunk):
                split_lo(first_chunk + 3, first_chunk + NK + 3)
                for t in range(NT):
                    residual(dst, arrived, count, first_panel, 0, t)
                split_lo(first_chunk + NK + 3, first_chunk + 2 * NK)
            first_residual(buf[1], x_again, 16, 4, FIRST_O0)
            dve.wait_ge(g1_loaded, 32)
            split_gates(16)
            for t in range(NT + 4):
                if t < NT:
                    residual(buf[1], x_again, 16, 4, 1, t)
                if 2 <= t < NT + 2:
                    normalise(1, buf[1], buf[0], t - 2)
                if t >= 4:
                    for m in range(2):
                        turn_lo(2, 2 * (t - 4) + m, t - 4, m)
            split_lo(FIRST_A, FIRST_A + 3)

            dve.wait_ge(gate_acc, 4)
            V.tensor_copy(g_in[:].rearrange("p (a b) -> p a b", a=2), bank[0:16, 0:2, :]).then_inc(gate_in, 1)
            dve.wait_ge(ml_loaded, 16)
            dve.wait_ge(gate_moved, 16)
            fg, tmp, b_row, u_row, m_row = (g[:] for g in gr)

            def chunks(r):
                return r.rearrange("p (c t) -> p c t", c=NT)
            log_gate(fg, tmp, fg, gate_b[:, 2:3], 2)
            step(V.tensor_tensor_scan(b_row, reset[:], fg, 0.0, ALU.mult, ALU.add))
            step(V.scalar_tensor_tensor(out=u_row, in0=g_in[0:8, :], scalar=gate_b[:, 1:2], in1=b_row,
                                        op0=ALU.add, op1=ALU.subtract))
            step(V.memset(tmp, 0.0))
            step(V.tensor_copy(chunks(tmp)[:, 1:NT, 0], chunks(b_row)[:, 0:NT - 1, P - 1]))
            step(V.tensor_tensor_scan(m_row, tmp, u_row, 0.0, ALU.add, ALU.max))
            V.tensor_scalar(tmp, m_row, -1.0, None, ALU.mult).then_inc(neg_ready, 1)
            step(V.memset(lrow[:], 0.0))
            step(V.tensor_tensor(lrow[:, 1:NT, 8], chunks(m_row)[:, 0:NT - 1, P - 1],
                                 chunks(b_row)[:, 0:NT - 1, P - 1], ALU.add))
            step(V.tensor_tensor(lrow[:, :, 9], lrow[:, :, 8], chunks(m_row)[:, :, P - 1], ALU.subtract))
            step(V.tensor_tensor(lrow[:, :, 0:8], lrow[:, :, 9:10].broadcast_to([8, NT, 8]),
                                 ident[0:8, 0:8].unsqueeze(1).broadcast_to([8, NT, 8]), ALU.mult))
            step(V.memset(rows4[:], 0.0))
            V.tensor_copy(rows4[0:8, :], u_row)
            V.tensor_tensor(chunks(rows4[32:40, :]), lrow[:, :, 8:9].broadcast_to([8, NT, P]), chunks(m_row),
                            ALU.subtract)
            V.scalar_tensor_tensor(out=rows4[64:72, :], in0=b_row, scalar=-1.0, in1=m_row, op0=ALU.mult,
                                   op1=ALU.subtract)
            V.tensor_tensor(chunks(rows4[96:104, :]), chunks(u_row),
                            chunks(m_row)[:, :, P - 1:P].broadcast_to([8, NT, P]), ALU.subtract)
            V.memset(ones8[:], 1.0).then_inc(gate_l, 1)
            dve.wait_ge(x1_stored, 16 * NT)
            V.memset(v_rows[:, :, :, P:P + 2], 1.0)
            panel_stage(6, FIRST_A, 4)
            split_lo(FIRST_B, FIRST_B + 3)

            def gate_product(p, t):
                if p >= 2:
                    dve.wait_ge(bank_free, taken(10 + p, t))
                    d = gl_rows[:, t, (p - 2) * PANEL:(p - 1) * PANEL]
                    V.tensor_tensor(d, d, zs[:, t % 2, :], ALU.mult).then_inc(gl_ready, 1)

            panel_stage(10, FIRST_B, 4, gate_product)
            split_lo(FIRST_O1, FIRST_O1 + 3)
            dve.wait_ge(acc_ready, 8 * 14)
            V.memset(state[:], 0.0).then_inc(ml_init, 1)

            def cell_sd(c):
                dve.wait_ge(d_ready, c + 1)
                for r in range(2):
                    dve.wait_ge(s_in, 2 * c + r + 1)
                    if c > 1:
                        dve.wait_ge(inter_in, 2 * (c - 1))
                    V.tensor_tensor(sd[2 * (c % 2) + r][:], bank[:, 2 + r, :].rearrange("p (h t) -> p h t", h=4),
                                    decay[c % 3][:, r:8:2, :], ALU.mult).then_inc(sd_ready, 1)

            def cell_take(c, mm):
                dve.wait_ge(inter_in, 2 * c + mm + 1)
                num = bank[:, 4 + 2 * mm:6 + 2 * mm, 0:258].rearrange("p r (i e) -> p r i e", i=2)
                floor = cols[:, c, 2, 4 * mm:4 * mm + 4].rearrange("p (i r) -> p r i", r=2)
                step(V.tensor_scalar(den[:, mm, 0], num[:, :, :, P], -1.0, None, ALU.mult))
                step(V.tensor_tensor(den[:, mm, 1], num[:, :, :, P], den[:, mm, 0], ALU.max))
                step(V.tensor_tensor(den[:, mm, 2], den[:, mm, 1], floor, ALU.max))
                step(V.reciprocal(den[:, mm, 0], den[:, mm, 2]))
                for i in range(2):
                    V.scalar_tensor_tensor(out=state[:, 2 * mm + i, 0:129], in0=state[:, 2 * mm + i, 0:129],
                                           scalar=w_old[:, c, 2 * mm + i:2 * mm + i + 1],
                                           in1=bank[:, 4 + 2 * mm + i, 258:387], op0=ALU.mult, op1=ALU.add)
                for i in range(2):
                    for r in range(2):
                        h = 4 * mm + 2 * i + r
                        y = gl_rows[:, c, h * P:(h + 1) * P]
                        last = V.scalar_tensor_tensor(out=y, in0=num[:, r, i, 0:P], scalar=den[:, mm, 0, r, i:i + 1],
                                                      in1=y, op0=ALU.mult, op1=ALU.mult)
                last.then_inc(state_ready, 1)

            cell_sd(0)
            for c in range(NT):
                cell_take(c, 0)
                if c + 1 < NT:
                    cell_sd(c + 1)
                cell_take(c, 1)
            for t in range(NT):
                for m in range(2):
                    turn_lo(3, 2 * t + m, t, m)
            first_residual(buf[0], tile_loaded, 32, 14, FIRST_O1)
            dve.wait_ge(g2_loaded, 16)
            for t in range(NT + 2):
                if t < NT:
                    residual(buf[0], tile_loaded, 32, 14, 1, t)
                if t >= 2:
                    normalise(2, buf[0], buf[1], t - 2)

        @block.gpsimd
        def _(pool):
            G = nc.gpsimd
            steps = [0]

            def step(ins):
                steps[0] += 1
                ins.then_inc(pool_chain, 1)
                pool.wait_ge(pool_chain, steps[0])


            def rstd(n, parts):
                for t in range(NT):
                    pool.wait_ge(squares_ready, squares_of(n, t))
                    if parts == 2:
                        step(G.tensor_tensor(stat[:, 0, t:t + 1], stat[:, 0, t:t + 1], stat[:, 3, t:t + 1], ALU.add))
                    G.tensor_scalar(stat[:, 1, t:t + 1], stat[:, 0, t:t + 1], 1.0 / D_MODEL, EPS, ALU.mult,
                                    ALU.add).then_inc(mean_ready, 1)
                    pool.wait_ge(mean_ready, NT * n + t + 1)
                    G.tensor_tensor(stat[:, 2, t:t + 1], stat[:, 1, t:t + 1], neg_half[:, 0:1],
                                    ALU.pow).then_inc(rstd_ready, 1)

            step(G.memset(neg_half[:], -0.5))
            rstd(0, 1)
            pool.wait_ge(f_ready, 1)
            pool.dma_start(f_scr, f_parts[:]).then_inc(f_stored, 16)
            for p in range(2):
                for t in range(NT):
                    pool.wait_ge(bank_free, taken(p, t))
                    pool.dma_start(v_scr[t * P:(t + 1) * P, p * PANEL:(p + 1) * PANEL],
                                   v_stage[:, t, :]).then_inc(v_stored[t], 16)

            def load_pair(u):
                kind, j = u % 2, u // 2
                src = v_scr.rearrange("(t p) d -> p t d", p=P)
                if kind:
                    pool.dma_start(v_pair[1][:, :, 0:P],
                                   src[:, :, FOX_WIDTH + P * j:FOX_WIDTH + P * (j + 1)]).then_inc(v_loaded[1], 16)
                else:
                    for a in range(2):
                        pool.dma_start(v_pair[0][:, :, 65 * a:65 * a + 64],
                                       src[:, :, P * j + 64 * a:P * j + 64 * a + 64]).then_inc(v_loaded[0], 16)
                        pool.dma_start(k_b[0][a][64:66, :], f_scr[2 * j + a]).then_inc(rowf_loaded, 16)

            for t in range(NT):
                pool.wait_ge(v_stored[t], 32)
            pool.wait_ge(helper_init, 1)
            pool.wait_ge(helper_sub, 1)
            pool.wait_ge(f_stored, 16)
            load_pair(0)

            def twice(u, g):
                kind, half = u % 2, slice((g % 2) * PANEL, (g % 2 + 1) * PANEL)
                for a in range(2):
                    r, other = slice(64 * a, 64 * a + 64), slice(64 - 64 * a, 128 - 64 * a)
                    pool.wait_ge(qk_hi, 2 * (4 * u + g) + a + 1)
                    if g < 2:
                        src, dst = q_a[kind][a][r, half], q_a[kind][a][other, half]
                    else:
                        src, dst = k_a[kind][a][r, half], k_b[kind][a][0:64, half]
                    G.tensor_copy(dst, src).then_inc(qk_twice, 1)
                    pool.wait_ge(qk_twice, 2 * (4 * u + g) + a + 1)

            for g in range(4):
                twice(0, g)
            o_rows = o_scr.rearrange("(t p) d -> p t d", p=P)
            for u in range(PAIRS):
                kind, j = u % 2, u // 2
                if u + 1 < PAIRS:
                    if u > 0:
                        pool.wait_ge(pv_ready, 8 * u)
                    load_pair(u + 1)
                if u + 1 < PAIRS:
                    for g in range(4):
                        twice(u + 1, g)
                pool.wait_ge(pv_free, 8 * (u + 1))
                o = o_pair[kind]
                if kind:
                    pool.wait_ge(o_squares, NT * (j + 1))
                    step(G.tensor_scalar(sub_ss[:, 1, :], sub_ss[:, 0, :], 1.0 / P, EPS, ALU.mult, ALU.add))
                    step(G.tensor_tensor(sub_ss[:, 0, :], sub_ss[:, 1, :], neg_half[:], ALU.pow))
                    step(G.tensor_tensor(o[:], o[:], sub_ss[:, 0, :].unsqueeze(2).broadcast_to([P, NT, P]), ALU.mult))
                    step(G.tensor_tensor(o[:], o[:], sub_g[:].unsqueeze(1).broadcast_to([P, NT, P]), ALU.mult))
                pool.dma_start(o_rows[:, :, FOX_WIDTH * kind + P * j:FOX_WIDTH * kind + P * (j + 1)],
                               o[:]).then_inc(o_stored[kind], 16)

            for c in range(2):
                pool.wait_ge(o_stored[c], 16 * PAIRS // 2)
            for t in range(NT):
                pool.dma_start(buf[0][:, t, :], o_scr[t * P:(t + 1) * P, :]).then_inc(o_loaded[t], 16)
            rstd(1, 2)

            def cell_mask(c):
                pool.wait_ge(m_loaded[c % 3], 16 * (c // 3 + 1))
                G.tensor_tensor(decay[c % 3][:], decay[c % 3][:],
                                mask_k[:].bitcast(F32).unsqueeze(1).broadcast_to([P, ML_HEADS, P]),
                                ALU.add).then_inc(mask_ready, 1)

            def cell_weighted(c):
                if c > 0:
                    pool.wait_ge(qd_turned, c)
                G.tensor_tensor(q_decayed[:], qk_rows[:, c, 0:PANEL].rearrange("p (h d) -> p h d", h=8),
                                cols[:, c, 1, :].unsqueeze(2).broadcast_to([P, 8, ML_QK]),
                                ALU.mult).then_inc(qd_ready, 1)
                if c > 1:
                    pool.wait_ge(inter_in, 2 * (c - 1))
                G.tensor_tensor(kw[c % 2][:], qk_rows[:, c, PANEL:2 * PANEL].rearrange("p (h d) -> p h d", h=8),
                                cols[:, c, 3, :].unsqueeze(2).broadcast_to([P, 8, ML_QK]),
                                ALU.mult).then_inc(kw_ready, 1)

            pool.wait_ge(neg_ready, 1)
            pool.dma_start(m_scr, gr[1][:]).then_inc(m_stored, 16)
            pool.wait_ge(cols_ready, 3)
            cell_mask(0)
            cell_mask(1)
            pool.wait_ge(acc_ready, 8 * 14)
            cell_weighted(0)
            for c in range(NT):
                if c + 1 < NT:
                    cell_weighted(c + 1)
                if c + 2 < NT:
                    cell_mask(c + 2)
            rstd(2, 2)


def kernel(x, positions, attn_norm_g, attn_w_in, fox_b_f, diff_lam_q1, diff_lam_k1, diff_lam_q2, diff_lam_k2,
           diff_subln_g, attn_w_out, ml_norm_g, ml_w_in, ml_b_i, ml_b_f, ml_w_out, final_norm_g):
    import concourse.bacc as bacc
    from concourse.bass_utils import run_bass_kernel_spmd

    arrays = {
        "x": x, "positions": positions, "attn_norm_g": attn_norm_g, "attn_w_in": attn_w_in, "fox_b_f": fox_b_f,
        "lams": np.concatenate([np.asarray(a) for a in (diff_lam_q1, diff_lam_k1, diff_lam_q2, diff_lam_k2)], axis=1),
        "subln_g": diff_subln_g, "attn_w_out": attn_w_out, "ml_norm_g": ml_norm_g, "ml_w_in": ml_w_in,
        "ml_b": np.concatenate([np.asarray(ml_b_i), np.asarray(ml_b_f)], axis=0).T, "ml_w_out": ml_w_out,
        "final_norm_g": final_norm_g, "const": constants(),
    }
    arrays = {"in_" + k: np.ascontiguousarray(v) for k, v in arrays.items()}
    nc = bacc.Bacc("TRN2", target_bir_lowering=False, num_devices=1)
    args = [nc.dram_tensor(k, v.shape, mybir.dt.from_np(v.dtype), kind="ExternalInput").ap()
            for k, v in arrays.items()]
    args.append(nc.dram_tensor("out_y", (1, SEQ, D_MODEL), F32, kind="ExternalOutput").ap())
    build(nc, *args)
    return run_bass_kernel_spmd(nc, [arrays], core_ids=[0]).results[0]["out_y"]
```

```python
import math
from contextlib import ExitStack

import numpy as np

import concourse.bass as bass
from concourse import mybir

F32 = mybir.dt.float32
F32R = mybir.dt.float32r
I32 = mybir.dt.int32
ALU = mybir.AluOpType
ACT = mybir.ActivationFunctionType
AX = mybir.AxisListType

P = 128
SEQ = 1024
D_MODEL = 1024
NT = SEQ // P
NK = D_MODEL // P
PANEL = 512
RING = 4

HEAD_DIM = 64
FOX_HEADS = 8
DIFF_HEADS = 4
FOX_WIDTH = FOX_HEADS * HEAD_DIM
DIFF_WIDTH = DIFF_HEADS * 2 * HEAD_DIM
COL_FQ = 0
COL_FK = COL_FQ + FOX_WIDTH
COL_FV = COL_FK + FOX_WIDTH
COL_FF = COL_FV + FOX_WIDTH
COL_DQ = COL_FF + FOX_HEADS
COL_DK = COL_DQ + DIFF_WIDTH
COL_DV = COL_DK + DIFF_WIDTH
COL_AZ = COL_DV + DIFF_WIDTH

ML_HEADS = 8
ML_QK = 64
ML_V = 128
COL_MQ = 0
COL_MV = 2 * ML_HEADS * ML_QK
COL_MG = COL_MV + ML_HEADS * ML_V
COL_MO = COL_MG + 2 * ML_HEADS
COL_MZ = COL_MO + ML_HEADS * ML_V

EPS = 1e-6
NEG = -1.0e30
LAM_INIT = 0.8 - 0.6 * math.exp(-0.3 * 0)
TWO_PI_1 = 6.28125
TWO_PI_2 = 0.00193500518798828125
TWO_PI_3 = 2.0 * math.pi - TWO_PI_1 - TWO_PI_2
PI_SAFE = 3.1415925
ROUND = 12582912.0

PAIRS = 8
CHUNKS_V, CHUNKS_PAIRS, CHUNKS_PANEL = 2 * NK, PAIRS * 4, NK
FIRST_V = 0
FIRST_PAIRS = FIRST_V + CHUNKS_V
FIRST_Z = FIRST_PAIRS + CHUNKS_PAIRS
FIRST_O0 = FIRST_Z + 2 * NK
FIRST_A = FIRST_O0 + 2 * NK
FIRST_B = FIRST_A + 4 * NK
FIRST_O1 = FIRST_B + 4 * NK

C_IDENT, C_MASKQ, C_MASKK = (P * n for n in range(3))
C_INV = 3 * P
C_SIGN = C_INV + 1
C_EARLY = C_SIGN + 1
C_RESET = C_EARLY
C_COLS = C_RESET + SEQ


def constants():
    c = np.zeros((P, C_COLS), np.float32)
    i = np.arange(P)
    c[:, C_IDENT:C_IDENT + P] = np.eye(P)
    c[:, C_MASKQ:C_MASKQ + P] = np.where(i[None, :] > i[:, None], NEG, 0.0)
    c[:, C_MASKK:C_MASKK + P] = np.where(i[None, :] < i[:, None], NEG, 0.0)
    half = HEAD_DIM // 2
    inv = np.float32(10000.0) ** (-np.arange(half, dtype=np.float32) / np.float32(half))
    c[:, C_INV] = inv[i % half]
    c[:, C_SIGN] = np.where(i % HEAD_DIM < half, -1.0, 1.0)
    c[:, C_RESET:C_RESET + SEQ] = 1.0
    c[:, C_RESET:C_RESET + SEQ:P] = 0.0
    return c


MAX_CHUNKS = [(i, c * 4, min(i + 1 - 4 * c, 4)) for i in range(NT) for c in range(i // 4 + 1)]
EXP_CHUNKS = [(k, max(4 * g, k), 4 * g + 4) for g in range(2) for k in range(4 * g + 4)]
EXP_AT = {}
_at = 0
for _n, (_k, _a, _b) in enumerate(EXP_CHUNKS):
    EXP_AT[(_k, _a // 4)] = (_at - _a * P)
    _at += (_b - _a) * P
PT_COLS = _at


def build(nc, x, positions, attn_norm_g, attn_w_in, fox_b_f, lams, subln_g, attn_w_out,
          ml_norm_g, ml_w_in, ml_b, ml_w_out, final_norm_g, const, out):
    v_scr = nc.dram_tensor("v_scr", (SEQ, D_MODEL), F32).ap()
    o_scr = nc.dram_tensor("o_scr", (SEQ, D_MODEL), F32).ap()
    x1_scr = nc.dram_tensor("x1_scr", (SEQ, D_MODEL), F32).ap()
    m_scr = nc.dram_tensor("m_scr", (ML_HEADS, SEQ), F32).ap()
    f_scr = nc.dram_tensor("f_scr", (FOX_HEADS, 2, SEQ), F32R).ap()

    ctx = ExitStack()
    with ctx:
        def sb(name, shape, dt=F32, scope=ctx):
            return scope.enter_context(nc.sbuf_tensor(name, shape, dt))

        def sem(name):
            return ctx.enter_context(nc.semaphore(name))

        bank = ctx.enter_context(nc.psum_tensor("bank", [P, 8, PANEL], F32))

        w_raw = sb("w_raw", [P, RING, PANEL])
        w_hi = sb("w_hi", [P, RING, PANEL], F32R)
        w_lo = sb("w_lo", [P, RING, PANEL], F32R)
        ident = sb("ident", [P, P])
        ident_r = sb("ident_r", [P, P], F32R)
        mask_q = sb("mask_q", [P, P], F32R)
        mask_k = sb("mask_k", [P, P], F32R)
        gate_raw = sb("gate_raw", [P, NK, 16])
        stat = sb("stat", [P, 4, NT])
        neg_half = sb("neg_half", [P, NT])
        neg_lam = sb("neg_lam", [P, 1])
        gate_hi = sb("gate_hi", [P, NK, 16], F32R)
        gate_lo = sb("gate_lo", [P, NK, 16], F32R)
        gate_b = sb("gate_b", [8, 4])
        inv_sign = sb("inv_sign", [P, 2])

        ht_scope = ExitStack()
        ht_hi = sb("ht_hi", [P, NK, SEQ], F32R, ht_scope)
        ht_lo = sb("ht_lo", [P, NK, SEQ], F32R, ht_scope)

        att = ExitStack()
        q_a = [[sb(f"q_a{c}{a}", [P, SEQ], F32R, att) for a in range(2)] for c in range(2)]
        q_b = [[sb(f"q_b{c}{a}", [68, SEQ], F32R, att) for a in range(2)] for c in range(2)]
        k_a = [[sb(f"k_a{c}{a}", [P, SEQ], F32R, att) for a in range(2)] for c in range(2)]
        k_b = [[sb(f"k_b{c}{a}", [68, SEQ], F32R, att) for a in range(2)] for c in range(2)]
        cos_t = sb("cos_t", [P, SEQ], F32, att)
        sin_t = sb("sin_t", [P, SEQ], F32, att)
        v_pair = [sb(f"v_pair{c}", [P, NT, 130], F32, att) for c in range(2)]
        m_part = sb("m_part", [P, 2, 12], F32, att)
        m_max = sb("m_max", [P, 2, NT], F32, att)
        m_cols = sb("m_cols", [P, 2, 2, NT], F32R, att)
        m_rows = sb("m_rows", [2 * NT, 2, P], F32R, att)
        recip = sb("recip", [P, 2, 16], F32, att)
        sub_g = sb("sub_g", [P, P], F32, att)
        sub_ss = sb("sub_ss", [P, 2, NT], F32, att)
        c_work = ExitStack()
        c_raw = sb("c_raw", [P, C_EARLY], F32, c_work)
        turn = sb("turn", [P, SEQ], F32, c_work)
        angle = sb("angle", [P, SEQ], F32, c_work)
        pos_i = sb("pos_i", [P, SEQ], I32, c_work)
        c_work.close()
        sub_sq = sb("sub_sq", [P, 2, P], F32, att)
        o_pair = [sb(f"o_pair{c}", [P, NT, P], F32, att) for c in range(2)]
        work = ExitStack()
        probs = sb("probs", [P, PT_COLS], F32, work)
        qs = sb("qs", [P, PANEL], F32, work)
        rot = sb("rot", [P, PANEL], F32, work)
        work.close()
        v_work = ExitStack()
        below = sb("below", [P, C_EARLY + 3 * SEQ - 2 * P - 2 * NT * P], F32, v_work)
        row = [sb(f"row{n}", [8, SEQ], F32, v_work) for n in range(2)]
        f_parts = sb("f_parts", [8, 2, SEQ], F32R, v_work)
        lam_row = sb("lam_row", [1, 4 * HEAD_DIM + 8], F32, v_work)
        v_work.close()
        att.close()

        lay = ExitStack()
        buf = [sb(f"buf{n}", [P, NT, D_MODEL], F32, lay) for n in range(2)]
        silu = sb("silu", [P, 2, PANEL], F32, lay)
        pad = sb("pad", [P, SEQ], F32, lay)
        g_rows = sb("g_rows", [P, D_MODEL], F32, lay)
        lay.close()
        vs = ExitStack()
        v_stage = sb("v_stage", [P, NT, PANEL], F32, vs)
        vs.close()

        hid = ExitStack()
        qk_rows = sb("qk_rows", [P, NT, 2 * ML_HEADS * ML_QK], F32, hid)
        v_rows = sb("v_rows", [P, NT, ML_HEADS, 130], F32, hid)
        gl = ExitStack()
        gl_rows = sb("gl_rows", [P, NT, ML_HEADS * ML_V], F32, gl)
        gl.close()
        rw = ExitStack()
        g_in = sb("g_in", [16, SEQ], F32, rw)
        gr = [sb(f"gr{n}", [8, SEQ], F32, rw) for n in range(5)]
        rows4 = sb("rows4", [P, SEQ], F32, rw)
        reset = sb("reset", [8, SEQ], F32, rw)
        rw.close()
        gap = sb("gap", [P, NT * D_MODEL], F32, hid)
        decay = [sb(f"decay{n}", [P, ML_HEADS, P], F32, hid) for n in range(3)]
        cols = sb("cols", [P, NT, 4, 8], F32, hid)
        w_old = sb("w_old", [P, NT, ML_HEADS], F32, hid)
        lrow = sb("lrow", [8, NT, 10], F32, hid)
        ones8 = sb("ones8", [8, P], F32, hid)
        zs = sb("zs", [P, 2, PANEL], F32, hid)
        hid.close()
        ht_scope.close()

        ml = ExitStack()
        q_t = [sb(f"q_t{n}", [P, 4, P], F32, ml) for n in range(2)]
        k_t = [sb(f"k_t{n}", [P, 4, P], F32, ml) for n in range(2)]
        kw = [sb(f"kw{n}", [P, ML_HEADS, ML_QK], F32, ml) for n in range(2)]
        qd_t = [sb(f"qd_t{n}", [P, 4, P], F32, ml) for n in range(2)]
        q_decayed = sb("q_decayed", [P, ML_HEADS, ML_QK], F32, ml)
        sd = [sb(f"sd{n}", [P, 4, P], F32, ml) for n in range(4)]
        state = sb("state", [P, 4, 130], F32, ml)
        den = sb("den", [P, 2, 3, 2, 2], F32, ml)
        ml.close()

        raw_loaded = [sem(f"raw_loaded{n}") for n in range(RING)]
        v_stored = [sem(f"v_stored{n}") for n in range(NT)]
        v_loaded = [sem(f"v_loaded{n}") for n in range(2)]
        o_stored = [sem(f"o_stored{n}") for n in range(2)]
        tile_loaded = [sem(f"tile_loaded{n}") for n in range(NT)]
        hi_split = sem("hi_split")
        w_ready = sem("w_ready")
        w_used = sem("w_used")
        acc_ready = sem("acc_ready")
        bank_free = sem("bank_free")
        turned = sem("turned")
        turned_hi = sem("turned_hi")
        turned_lo = sem("turned_lo")
        consts_loaded = sem("consts_loaded")
        consts_ready = sem("consts_ready")
        squares_ready = sem("squares_ready")
        mean_ready = sem("mean_ready")
        rstd_ready = sem("rstd_ready")
        xn_ready = sem("xn_ready")
        xg_ready = sem("xg_ready")
        xs_ready = sem("xs_ready")
        g_loaded = sem("g_loaded")
        small_loaded = sem("small_loaded")
        gate_acc = sem("gate_acc")
        dve_chain = sem("dve_chain")
        pool_chain = sem("pool_chain")
        gate_e = sem("gate_e")
        gate_u = sem("gate_u")
        gate_l = sem("gate_l")
        f_ready = sem("f_ready")
        f_stored = sem("f_stored")
        rowf_loaded = sem("rowf_loaded")
        pos_loaded = sem("pos_loaded")
        rope_args = sem("rope_args")
        rope_ready = sem("rope_ready")
        lam_loaded = sem("lam_loaded")
        lam_sum = sem("lam_sum")
        gate_split = sem("gate_split")
        lam_exp = sem("lam_exp")
        lam_one = sem("lam_one")
        lam_bc = sem("lam_bc")
        lam_ready = sem("lam_ready")
        proj_done = sem("proj_done")
        pj_copied = sem("pj_copied")
        pj_free = sem("pj_free")
        roped = sem("roped")
        qk_hi = sem("qk_hi")
        qk_ready = sem("qk_ready")
        qk_twice = sem("qk_twice")
        max_in = sem("max_in")
        max_done = sem("max_done")
        m_ready = sem("m_ready")
        m_turned = sem("m_turned")
        m_copied = sem("m_copied")
        m_moved = [sem(f"m_moved{n}") for n in range(2)]
        exp_in = sem("exp_in")
        probs_ready = sem("probs_ready")
        pv_ready = sem("pv_ready")
        pv_free = sem("pv_free")
        o_loaded = [sem(f"o_loaded{n}") for n in range(NT)]
        x_again = [sem(f"x_again{n}") for n in range(NT)]
        o_squares = sem("o_squares")
        helper_init = sem("helper_init")
        y_ready = sem("y_ready")
        x1_stored = sem("x1_stored")
        gate_moved = sem("gate_moved")
        gate_in = sem("gate_in")
        cols_turned = sem("cols_turned")
        cols_ready = sem("cols_ready")
        wold_bc = sem("wold_bc")
        ml_loaded = sem("ml_loaded")
        ml_init = sem("ml_init")
        gate_exp = sem("gate_exp")
        gate_ln = sem("gate_ln")
        helper_sub = sem("helper_sub")
        q_turned = sem("q_turned")
        k_turned = sem("k_turned")
        q_ready = sem("q_ready")
        k_ready = sem("k_ready")
        s_in = sem("s_in")
        neg_ready = sem("neg_ready")
        m_stored = sem("m_stored")
        m_loaded = [sem(f"m_loaded{n}") for n in range(3)]
        qd_ready = sem("qd_ready")
        qd_turned = sem("qd_turned")
        qd_copied = sem("qd_copied")
        kw_ready = sem("kw_ready")
        mask_ready = sem("mask_ready")
        d_ready = sem("d_ready")
        sd_ready = sem("sd_ready")
        inter_in = sem("inter_in")
        state_ready = sem("state_ready")
        out_stored = sem("out_stored")
        g1_loaded = sem("g1_loaded")
        g2_loaded = sem("g2_loaded")
        gl_ready = sem("gl_ready")

        def panels(e, n, body):
            if n > 2:
                with e.Fori(0, n) as p:
                    body(p)
            else:
                for p in range(n):
                    body(p)

        chunk_used, used = [], 0
        for n in range(FIRST_O1 + 2 * NK):
            if FIRST_PAIRS <= n < FIRST_Z:
                last = n % 2 == 1
                signal = (proj_done, 2 * ((n - FIRST_PAIRS) // 2 + 1))
            else:
                last = n % NK == NK - 1
                done = n + 1 if n < FIRST_PAIRS else n + 1 - CHUNKS_PAIRS
                signal = (acc_ready, done)
            if not last:
                used += 1
                signal = (w_used, used)
            chunk_used.append(signal)

        def taken(panel, t):
            return 8 + 8 * panel + t + 1

        def squares_of(n, t):
            return t + 1 if n == 0 else 16 * n + t + 1

        block = ctx.enter_context(nc.Block())

        @block.sync
        def _(sp):
            xt = x[0].rearrange("(t p) d -> t p d", p=P)
            sp.dma_start(c_raw[:], const[:, 0:C_EARLY]).then_inc(consts_loaded, 16)
            sp.dma_start(buf[0][:, 0, :], xt[0]).then_inc(tile_loaded[0], 16)
            sp.dma_start(lam_row[:, 0:4 * HEAD_DIM], lams).then_inc(lam_loaded, 16)
            sp.dma_start(g_rows[:], attn_norm_g[0:1, :].broadcast_to([P, D_MODEL])).then_inc(g_loaded, 16)
            for t in range(1, NT):
                sp.dma_start(buf[0][:, t, :], xt[t]).then_inc(tile_loaded[t], 16)
            sp.dma_start(gate_raw[:, :, 0:8], attn_w_in[0][:, COL_FF:COL_FF + 8].rearrange("(k p) c -> p k c", p=P)).then_inc(small_loaded, 16)
            sp.dma_start(gate_b[:, 0:1], fox_b_f.rearrange("a h -> h a")).then_inc(small_loaded, 16)
            sp.dma_start(gate_b[:, 1:3], ml_b).then_inc(small_loaded, 16)
            sp.dma_start(sub_g[:], subln_g[0:1, :].broadcast_to([P, P])).then_inc(small_loaded, 16)
            sp.dma_start(pos_i[:], positions[0:1, :].broadcast_to([P, SEQ])).then_inc(pos_loaded, 16)

            def chunk(n, src):
                if n + 1 - RING > 0:
                    sp.wait_ge(w_ready, n + 1 - RING)
                sp.dma_start(w_raw[:, n % RING, :], src).then_inc(raw_loaded[n % RING], 16)

            def load_panels(first, n, w, col, stride, lo=0):
                for i in range(lo, n * NK):
                    p, k = divmod(i, NK)
                    c = col + p * stride
                    chunk(first + i, w[k * P:(k + 1) * P, c:c + PANEL])

            def load_first(first, w, col):
                for k in range(RING):
                    chunk(first + k, w[k * P:(k + 1) * P, col:col + PANEL])

            load_panels(FIRST_V, 2, attn_w_in[0], COL_FV, COL_DV - COL_FV)
            def load_pair_half(u, i):
                if u < PAIRS:
                    c = ((COL_FQ, COL_FK), (COL_DQ, COL_DK))[u % 2][i] + P * (u // 2)
                for g in range(2):
                    n = FIRST_PAIRS + 4 * u + 2 * i + g
                    if u == PAIRS:
                        k = 2 * i + g
                        chunk(n, attn_w_in[0][k * P:(k + 1) * P, COL_AZ:COL_AZ + PANEL])
                    else:
                        src = attn_w_in[0][g * 512:(g + 1) * 512, c:c + P]
                        sp.wait_ge(w_ready, n + 1 - RING)
                        sp.dma_start(w_raw[:, n % RING, :].rearrange("p (k c) -> p k c", k=4),
                                     src.rearrange("(k p) c -> p k c", p=P)).then_inc(raw_loaded[n % RING], 16)
            for u in range(2):
                load_pair_half(u, 0)
                load_pair_half(u, 1)
            load_pair_half(2, 0)
            for u in range(PAIRS):
                if u + 2 <= PAIRS:
                    load_pair_half(u + 2, 1)
                if u + 3 <= PAIRS:
                    load_pair_half(u + 3, 0)
            load_panels(FIRST_Z, 2, attn_w_in[0], COL_AZ, PANEL, RING)
            sp.wait_ge(pv_free, 8 * PAIRS)
            for t in range(NT):
                sp.dma_start(buf[1][:, t, :], xt[t]).then_inc(x_again[t], 16)
            sp.dma_start(g_rows[:], ml_norm_g[0:1, :].broadcast_to([P, D_MODEL])).then_inc(g1_loaded, 16)
            sp.wait_ge(gate_acc, 2)
            sp.dma_start(gate_raw[:], ml_w_in[0][:, COL_MG:COL_MG + 16].rearrange("(k p) c -> p k c", p=P)).then_inc(g1_loaded, 16)
            load_panels(FIRST_O0, 2, attn_w_out[0], 0, PANEL)
            load_first(FIRST_A, ml_w_in[0], COL_MQ)
            for t in range(NT):
                sp.wait_ge(bank_free, taken(5, t))
                sp.dma_start(x1_scr[t * P:(t + 1) * P, :], buf[1][:, t, :]).then_inc(x1_stored, 16)
            sp.wait_ge(turned, 48)
            sp.dma_start(reset[:], const[0:8, C_RESET:C_RESET + SEQ]).then_inc(ml_loaded, 16)
            sp.wait_ge(gate_in, 1)
            sp.dma_start(gr[0][:], g_in[8:16, :]).then_inc(gate_moved, 16)
            load_panels(FIRST_A, 4, ml_w_in[0], COL_MQ, PANEL, RING)
            def load_neg_m(c):
                sp.dma_start(decay[c % 3][:], m_scr[:, c * P:(c + 1) * P].unsqueeze(0).broadcast_to(
                    [P, ML_HEADS, P])).then_inc(m_loaded[c % 3], 16)
            sp.wait_ge(m_stored, 16)
            for c in range(3):
                load_neg_m(c)
            load_panels(FIRST_B, 4, ml_w_in[0], COL_MO, PANEL)
            load_first(FIRST_O1, ml_w_out[0], 0)
            for c in range(3, NT):
                sp.wait_ge(sd_ready, 2 * (c - 2))
                load_neg_m(c)
            sp.wait_ge(kw_ready, NT)
            sp.wait_ge(qd_ready, NT)
            sp.wait_ge(k_turned, NT)
            sp.wait_ge(x1_stored, 16 * NT)
            for t in range(NT):
                sp.dma_start(buf[0][:, t, :], x1_scr[t * P:(t + 1) * P, :]).then_inc(tile_loaded[t], 16)
            sp.wait_ge(turned, 64)
            sp.dma_start(g_rows[:], final_norm_g.rearrange("(a d) -> a d", a=1).broadcast_to([P, D_MODEL])).then_inc(g2_loaded, 16)
            load_panels(FIRST_O1, 2, ml_w_out[0], 0, PANEL, RING)
            ot = out[0].rearrange("(t p) d -> t p d", p=P)
            for t in range(NT):
                sp.wait_ge(xn_ready, 2 * NT + t + 1)
                sp.wait_ge(xs_ready, NT + t + 1)
                sp.dma_start(ot[t], buf[1][:, t, :]).then_inc(out_stored, 16)
            sp.wait_ge(out_stored, 16 * NT)

        @block.tensor
        def _(pe):
            def turn_half(stage, n, src, t, m):
                if n >= 8:
                    pe.wait_ge(turned_lo, 16 * stage + n - 7)
                for k in range(4):
                    last = pe.transpose(bank[:, n % 8, k * P:(k + 1) * P],
                                        src[:, t, (4 * m + k) * P:(4 * m + k + 1) * P], ident[:])
                last.then_inc(turned, 1)

            def turn_tiles(stage, src, ready, base):
                for t in range(NT):
                    pe.wait_ge(ready, base + t + 1)
                    for m in range(2):
                        turn_half(stage, 2 * t + m, src, t, m)

            def gates(stage, width):
                for n in range(2):
                    pe.wait_ge(turned_lo, 16 * stage + 9 + 7 * n)
                    for k in range(NK):
                        for g, part in ((gate_hi, ht_hi), (gate_lo, ht_hi), (gate_hi, ht_lo)):
                            last = pe.matmul(bank[0:width, n, :], g[:, k, 0:width],
                                             part[:, k, n * PANEL:(n + 1) * PANEL],
                                             start=(k == 0 and g is gate_hi and part is ht_hi),
                                             stop=(k == NK - 1 and part is ht_lo))
                    last.then_inc(gate_acc, 1)

            def panel_products(first_panel, first_chunk, n, stage=None):
                def body(p):
                    for k in range(NK):
                        slot = k % RING
                        pe.wait_ge(w_ready, p * NK + (first_chunk + k + 1))
                        for t in range(NT):
                            if k == 0:
                                pe.wait_ge(bank_free, p * 8 + (first_panel * 8 + t + 1))
                                if stage is not None and p == 0:
                                    pe.wait_ge(turned_lo, 16 * stage + 8 + t + 1)
                            acc = bank[:, t, :]
                            hi, lo = ht_hi[:, k, t * P:(t + 1) * P], ht_lo[:, k, t * P:(t + 1) * P]
                            pe.matmul(acc, hi, w_hi[:, slot, :], start=(k == 0), stop=False)
                            pe.matmul(acc, hi, w_lo[:, slot, :], start=False, stop=False)
                            last = pe.matmul(acc, lo, w_hi[:, slot, :], start=False, stop=(k == NK - 1))
                            if k == NK - 1 and t < NT - 1:
                                last.then_inc(acc_ready, 1)
                        last.then_inc(acc_ready if k == NK - 1 else w_used, 1)
                panels(pe, n, body)

            pe.sem_inc(bank_free, 8)
            pe.wait_ge(consts_ready, 1)
            turn_tiles(0, buf[1], xn_ready, 0)
            pe.wait_ge(lam_one, 1)
            pe.wait_ge(turned_lo, 11)
            pe.matmul(bank[:, 2, 0:1], lam_row[:, 0:P], lam_row[:, 4 * HEAD_DIM + 5:4 * HEAD_DIM + 6],
                      start=True, stop=True).then_inc(lam_bc, 1)
            pe.wait_ge(gate_split, 1)
            gates(0, 8)
            pe.wait_ge(gate_u, 1)
            pe.wait_ge(lam_ready, 1)
            panel_products(0, FIRST_V, 2)

            def proj_steps(u, lo, hi):
                for n in range(lo, hi):
                    g, r = n // 24, n % 24
                    k, part = r // 3, r % 3
                    half, i = g % 2, g // 2
                    slot = 2 * i + k // 4
                    first = FIRST_PAIRS + 4 * u
                    if r == 0:
                        before_u, before_g = divmod(4 * u + g - 2, 4)
                        if before_u >= 0 and before_u % 2:
                            pe.wait_ge(pj_free, 4 * (before_u // 2) + before_g + 1)
                        else:
                            if 4 * u + g - 1 > 0:
                                pe.wait_ge(qk_ready, 4 * u + g - 1)
                    if r % 12 == 0:
                        pe.wait_ge(w_ready, first + slot + 1)
                    w = (w_hi, w_hi, w_lo)[part][:, slot, (k % 4) * P:(k % 4 + 1) * P]
                    h = (ht_hi, ht_lo, ht_hi)[part][:, k, half * PANEL:(half + 1) * PANEL]
                    last = pe.matmul(bank[:, g % 2, :], w, h, start=(r == 0), stop=(r == 23))
                    if r == 23:
                        last.then_inc(proj_done, 1)
                    if half == 1 and r == 11:
                        last.then_inc(w_used, 1)

            pe.wait_ge(bank_free, taken(1, 7))
            proj_steps(0, 0, 96)

            for u in range(PAIRS):
                kind, nxt = u % 2, u + 1
                fill = [0]

                def filler(n):
                    if nxt < PAIRS:
                        proj_steps(nxt, fill[0], fill[0] + n)
                        fill[0] += n

                rows_max, rows_exp = (66, 68) if kind == 0 else (64, 66)
                QA, QB, KA, KB = q_a[kind], q_b[kind], k_a[kind], k_b[kind]

                def max_products(a, lo, hi, fill_n):
                    for n in range(lo, hi):
                        i, k0, w = MAX_CHUNKS[n]
                        if a == 0 and n < 4:
                            if u > 0:
                                pe.wait_ge(probs_ready, 24 * u - 3 + n)
                        else:
                            pe.wait_ge(max_done, 24 * u + 12 * a + n - 3)
                        acc = bank[:, 2 + n % 4, :]
                        qt, kt = slice(i * P, (i + 1) * P), slice(k0 * P, (k0 + w) * P)
                        diag = i < k0 + w
                        pe.matmul(acc[:, 0:w * P], QA[a][:, qt], KA[a][:, kt], start=True, stop=False)
                        last = pe.matmul(acc[:, 0:w * P], QB[a][0:rows_max, qt], KB[a][0:rows_max, kt],
                                         start=False, stop=not diag)
                        if diag:
                            last = pe.matmul(acc[:, (i - k0) * P:(i - k0 + 1) * P], ident_r[:], mask_q[:],
                                             start=False, stop=True)
                        last.then_inc(max_in, 1)
                        filler(fill_n)

                def turn_maximum(a):
                    pe.wait_ge(m_ready, 2 * u + a + 1)
                    if u > 0:
                        pe.wait_ge(pv_free, 8 * u)
                    pe.transpose(bank[0:2 * NT, 6 + a, 3 * P:4 * P],
                                 m_cols[:, a].rearrange("p j t -> p (j t)").bitcast(F32), ident[:]).then_inc(m_turned, 1)

                def exp_products(a, lo, hi, fill_n):
                    for n in range(lo, hi):
                        if n == 0:
                            pe.wait_ge(m_moved[a], 32 * (u + 1))
                        k, t0, t1 = EXP_CHUNKS[n]
                        if a == 0 and n < 4:
                            pe.wait_ge(max_done, 24 * u + 21 + n)
                        else:
                            pe.wait_ge(probs_ready, 24 * u + 12 * a + n - 3)
                        acc = bank[:, 2 + n % 4, :]
                        kt, qt = slice(k * P, (k + 1) * P), slice(t0 * P, t1 * P)
                        w = (t1 - t0) * P
                        pe.matmul(acc[:, 0:w], KA[a][:, kt], QA[a][:, qt], start=True, stop=False)
                        last = pe.matmul(acc[:, 0:w], KB[a][0:rows_exp, kt], QB[a][0:rows_exp, qt],
                                         start=False, stop=k != t0)
                        if k == t0:
                            last = pe.matmul(acc[:, 0:P], ident_r[:], mask_k[:], start=False, stop=True)
                        last.then_inc(exp_in, 1)
                        filler(fill_n)

                def value_products(a, lo, hi):
                    width = 65 if kind == 0 else 129
                    v0 = 65 * a if kind == 0 else 0
                    for b in range(lo, hi):
                        pe.wait_ge(probs_ready, 24 * u + 12 * a + (4 if b < 2 else 12))
                        if 8 * u + 4 * a + b - 1 > 0:
                            pe.wait_ge(pv_free, 8 * u + 4 * a + b - 1)
                        for i in (2 * b, 2 * b + 1):
                            for k in range(i + 1):
                                at = EXP_AT[(k, i // 4)] + i * P
                                last = pe.matmul(bank[:, 6 + b % 2, (i % 2) * width:(i % 2 + 1) * width],
                                                 probs[:, at:at + P], v_pair[kind][:, k, v0:v0 + width],
                                                 start=(k == 0), stop=(k == i))
                        last.then_inc(pv_ready, 1)

                pe.wait_ge(qk_ready, 4 * u + 4)
                pe.wait_ge(qk_twice, 8 * (u + 1))
                if kind == 0:
                    pe.wait_ge(rowf_loaded, 32 * (u // 2 + 1))
                max_products(0, 0, 12, 2)
                max_products(1, 0, 5, 2)
                turn_maximum(0)
                max_products(1, 5, 12, 2)
                filler(6)
                exp_products(0, 0, 3, 2)
                turn_maximum(1)
                exp_products(0, 3, 6, 2)
                exp_products(0, 6, 12, 4)
                pe.wait_ge(v_loaded[kind], 32 // (1 + kind) * (u // 2 + 1))
                pe.wait_ge(m_copied, 2 * u + 2)
                value_products(0, 0, 2)
                exp_products(1, 0, 3, 2)
                exp_products(1, 3, 4, 0)
                value_products(0, 2, 4)
                exp_products(1, 4, 10, 0)
                value_products(1, 0, 2)
                exp_products(1, 10, 12, 0)
                value_products(1, 2, 4)

            pe.wait_ge(pv_free, 8 * PAIRS)
            panel_products(2, FIRST_Z, 2)
            for m in range(2):
                for t in range(NT):
                    pe.wait_ge(bank_free, taken(3, t))
                    pe.wait_ge(y_ready, 8 * m + t + 1)
                    turn_half(1, 8 * m + t, buf[0], t, m)
            panel_products(4, FIRST_O0, 2, 1)
            for t in range(NT):
                if t < NT // 2:
                    pe.wait_ge(bank_free, taken(5, 2 * t + 1))
                pe.wait_ge(xs_ready, t + 1)
                turn_half(2, 2 * t, buf[0], t, 0)
                pe.wait_ge(xn_ready, NT + t + 1)
                turn_half(2, 2 * t + 1, buf[0], t, 1)
            pe.wait_ge(gate_split, 2)
            gates(2, 16)
            pe.wait_ge(gate_in, 1)
            panel_products(6, FIRST_A, 4)
            pe.wait_ge(bank_free, taken(9, 7))
            pe.wait_ge(gate_l, 1)
            for c in range(NT):
                last = pe.transpose(bank[:, c // 4, (c % 4) * 104:(c % 4) * 104 + 104],
                                    rows4[0:104, c * P:(c + 1) * P], ident[0:104, 0:104])
                if c % 4 == 3:
                    last.then_inc(cols_turned, 1)
            pe.matmul(bank[:, 2, 0:NT * ML_HEADS], ones8[:], lrow[:, :, 0:8], start=True,
                      stop=True).then_inc(wold_bc, 1)
            pe.wait_ge(cols_ready, 3)
            panel_products(10, FIRST_B, 4)
            pe.wait_ge(bank_free, taken(13, 7))

            def turn_rows(to, src):
                for m in range(4):
                    last = pe.transpose(bank[:, to, m * P:(m + 1) * P], src[:, m * P:(m + 1) * P], ident[:])
                return last

            def turn_qk(c):
                if c > 0:
                    pe.wait_ge(qd_copied, c)
                    pe.wait_ge(k_ready, c)
                turn_rows(0, qk_rows[:, c, 0:PANEL]).then_inc(q_turned, 1)
                turn_rows(1, qk_rows[:, c, PANEL:2 * PANEL]).then_inc(k_turned, 1)

            def turn_decayed(c):
                pe.wait_ge(q_ready, c + 1)
                pe.wait_ge(qd_ready, c + 1)
                turn_rows(0, q_decayed[:].rearrange("p h d -> p (h d)")).then_inc(qd_turned, 1)

            def cell_scores(c):
                pe.wait_ge(q_ready, c + 1)
                pe.wait_ge(k_ready, c + 1)
                for r in range(2):
                    if c > 0:
                        pe.wait_ge(sd_ready, 2 * (c - 1) + r + 1)
                    rows = slice(64 * r, 64 * r + 64)
                    for m in range(4):
                        last = pe.matmul(bank[:, 2 + r, m * P:(m + 1) * P], k_t[c % 2][rows, m, :],
                                         q_t[c % 2][rows, m, :], start=True, stop=True)
                    last.then_inc(s_in, 1)

            def cell_outputs(c, mm):
                banks = [4 + 2 * mm, 5 + 2 * mm]
                if c > 0:
                    pe.wait_ge(state_ready, 2 * (c - 1) + mm + 1)
                pe.wait_ge(sd_ready, 2 * c + 2)
                pe.wait_ge(qd_copied, c + 1)
                pe.wait_ge(kw_ready, c + 1)
                for i in range(2):
                    m = 2 * mm + i
                    for r in range(2):
                        pe.matmul(bank[:, banks[r], i * 129:(i + 1) * 129], sd[2 * (c % 2) + r][:, m, :],
                                  v_rows[:, c, 2 * m + r, 0:129], start=True, stop=False)
                    for r in range(2):
                        pe.matmul(bank[:, banks[r], i * 129:(i + 1) * 129],
                                  qd_t[c % 2][64 * r:64 * r + 64, m, :],
                                  state[64 * r:64 * r + 64, m, 0:129], start=False, stop=True)
                for i in range(2):
                    m = 2 * mm + i
                    for r in range(2):
                        last = pe.matmul(bank[64 * r:64 * r + 64, banks[i], 258:387],
                                         kw[c % 2][:, 2 * m + r, :], v_rows[:, c, 2 * m + r, 0:129],
                                         start=True, stop=True)
                last.then_inc(inter_in, 1)

            turn_qk(0)
            cell_scores(0)
            turn_decayed(0)
            pe.wait_ge(ml_init, 1)
            for c in range(NT):
                if c + 1 < NT:
                    turn_qk(c + 1)
                cell_outputs(c, 0)
                if c + 1 < NT:
                    cell_scores(c + 1)
                    turn_decayed(c + 1)
                cell_outputs(c, 1)
            pe.wait_ge(state_ready, 2 * NT)
            for t in range(NT):
                pe.wait_ge(state_ready, 2 * (t + 1))
                for m in range(2):
                    turn_half(3, 2 * t + m, gl_rows, t, m)
            panel_products(14, FIRST_O1, 2, 3)

        @block.scalar
        def _(act):
            def split_hi(lo, hi):
                for n in range(lo, hi):
                    act.wait_ge(raw_loaded[n % RING], 16 * (n // RING + 1))
                    if n >= RING:
                        producer, count = chunk_used[n - RING]
                        act.wait_ge(producer, count)
                    act.activation(w_hi[:, n % RING, :], w_raw[:, n % RING, :], ACT.Copy).then_inc(hi_split, 1)

            def turn_hi(stage, n, t, m):
                act.wait_ge(turned, 16 * stage + n + 1)
                act.activation(ht_hi[:, 4 * m:4 * m + 4, t * P:(t + 1) * P],
                               bank[:, n % 8, :].rearrange("p (k c) -> p k c", k=4),
                               ACT.Copy).then_inc(turned_hi, 1)

            def squares(src, junk, t, part, cols):
                act.activation(junk[:, t, cols], src[:, t, cols], ACT.Square,
                               accum_out=stat[:, part, t:t + 1]).then_inc(squares_ready, 1)

            def half_squares(first_panel, src, junk, p, t):
                act.wait_ge(bank_free, taken(first_panel + p, t))
                squares(src, junk, t, 3 * p, slice(p * PANEL, (p + 1) * PANEL))

            def scale_half(n, dst, t):
                act.wait_ge(xg_ready, NT * (n - 1) + t + 1)
                act.wait_ge(rstd_ready, NT * n + t + 1)
                act.activation(dst[:, t, 0:PANEL], dst[:, t, 0:PANEL], ACT.Copy,
                               scale=stat[:, 2, t:t + 1]).then_inc(xs_ready, 1)

            def panel_stage(first_panel, first_chunk, n, take=None, split=3):
                for p in range(n):
                    c = first_chunk + NK * p
                    split_hi(c + (split if p == 0 else 3), c + NK)
                    if p + 1 < n:
                        split_hi(c + NK, c + NK + 3)
                    for t in range(NT if take else 0):
                        act.wait_ge(acc_ready, 8 * (first_panel + p) + t + 1)
                        take(p, t)

            act.wait_ge(lam_sum, 1)
            act.activation(lam_row[:, 258:260], lam_row[:, 256:258], ACT.Exp).then_inc(lam_exp, 1)
            for t in range(NT + 2):
                if t < NT:
                    act.wait_ge(tile_loaded[t], 16)
                    squares(buf[0], buf[1], t, 0, slice(0, D_MODEL))
                if t >= 2:
                    for m in range(2):
                        turn_hi(0, 2 * (t - 2) + m, t - 2, m)
            split_hi(FIRST_V, FIRST_V + 3)
            act.wait_ge(gate_e, 1)
            act.activation(row[1][:], row[1][:], ACT.Exp, scale=-1.0).then_inc(gate_exp, 1)
            act.wait_ge(gate_exp, 1)
            act.activation(row[1][:], row[1][:], ACT.Ln, bias=1.0).then_inc(gate_ln, 1)

            def take_v(p, t):
                if 16 * p > 0:
                    act.wait_ge(v_stored[t], 16 * p)
                act.activation(v_stage[:, t, :], bank[:, t, :],
                               ACT.Copy).then_inc(bank_free, 1)
            split_hi(FIRST_V + 3, FIRST_V + 7)
            act.wait_ge(rope_args, 1)
            act.activation(sin_t[:], angle[:], ACT.Sin)
            act.activation(cos_t[:], turn[:], ACT.Sin).then_inc(rope_ready, 1)
            panel_stage(0, FIRST_V, 2, take_v, split=7)
            split_hi(FIRST_PAIRS, FIRST_PAIRS + 4)

            def swap_quarter(u, g, quarter):
                act.wait_ge(proj_done, 4 * u + g + 1)
                if 4 * (u // 2) + g > 0:
                    act.wait_ge(roped, 4 * (u // 2) + g)
                src, dst = 32 * (quarter ^ 1), 32 * quarter
                act.activation(qs[dst:dst + 32, :], bank[src:src + 32, g % 2, :], ACT.Copy).then_inc(pj_copied, 1)

            def round_group(u, g):
                kind, half = u % 2, slice((g % 2) * PANEL, (g % 2 + 1) * PANEL)
                if kind:
                    act.wait_ge(roped, 4 * (u // 2) + g + 1)
                else:
                    act.wait_ge(proj_done, 4 * u + g + 1)
                for a in range(2):
                    r = slice(64 * a, 64 * a + 64)
                    src = rot[r, :] if kind else bank[r, g % 2, :]
                    if u == 0:
                        twice = q_a[0][a][64 - 64 * a:128 - 64 * a, half] if g < 2 else k_b[0][a][0:64, half]
                        act.activation(twice, src, ACT.Copy).then_inc(qk_twice, 1)
                    act.activation((q_a if g < 2 else k_a)[kind][a][r, half], src,
                                   ACT.Copy).then_inc(qk_hi, 1)

            def head_squares(u):
                act.wait_ge(pv_free, 8 * (u + 1))
                for i in range(NT):
                    n = NT * (u // 2) + i
                    if n > 1:
                        act.wait_ge(o_squares, n - 1)
                    act.activation(sub_sq[:, i % 2, :], o_pair[1][:, i, :], ACT.Square,
                                   accum_out=sub_ss[:, 0, i:i + 1]).then_inc(o_squares, 1)

            for t in range(NT):
                act.wait_ge(v_stored[t], 32)
            act.wait_ge(helper_init, 1)
            for g in range(4):
                round_group(0, g)

            for u in range(PAIRS):
                nxt = u + 1
                more, after = nxt < PAIRS, u + 2 < PAIRS
                rotary = nxt % 2 == 1

                def exps(a, lo, hi):
                    for n in range(lo, hi):
                        k, t0, t1 = EXP_CHUNKS[n]
                        if n == 0:
                            if 8 * u + 4 * a - 2 > 0:
                                act.wait_ge(pv_ready, 8 * u + 4 * a - 2)
                        if n == 4:
                            if 8 * u + 4 * a > 0:
                                act.wait_ge(pv_ready, 8 * u + 4 * a)
                        act.wait_ge(exp_in, 24 * u + 12 * a + n + 1)
                        at = EXP_AT[(k, n // 4 and 1)] + t0 * P
                        act.activation(probs[:, at:at + (t1 - t0) * P], bank[:, 2 + n % 4, 0:(t1 - t0) * P],
                                       ACT.Exp, scale=HEAD_DIM ** -0.5).then_inc(probs_ready, 1)

                if u == 0:
                    split_hi(FIRST_PAIRS + 4, FIRST_PAIRS + 6)
                if more:
                    split_hi(FIRST_PAIRS + 4 * nxt + 2, FIRST_PAIRS + 4 * nxt + 4)
                if u and u % 2 == 0:
                    head_squares(u - 1)
                if more and rotary:
                    for quarter in range(4):
                        swap_quarter(nxt, 0, quarter)
                    exps(0, 0, 2)
                    round_group(nxt, 0)
                    for quarter in range(4):
                        swap_quarter(nxt, 1, quarter)
                        exps(0, 2 + quarter, 3 + quarter)
                    exps(0, 6, 7)
                    round_group(nxt, 1)
                    exps(0, 7, 8)
                    for quarter in range(4):
                        exps(0, 8 + quarter, 9 + quarter)
                        swap_quarter(nxt, 2, quarter)
                elif more:
                    round_group(nxt, 0)
                    round_group(nxt, 1)
                    exps(0, 0, 8)
                    round_group(nxt, 2)
                    exps(0, 8, 12)
                else:
                    exps(0, 0, 12)
                if after:
                    split_hi(FIRST_PAIRS + 4 * (u + 2), FIRST_PAIRS + 4 * (u + 2) + 2)
                if u == PAIRS - 1:
                    split_hi(FIRST_Z, FIRST_Z + 3)
                exps(1, 0, 4)
                if more and rotary:
                    round_group(nxt, 2)
                    for quarter in range(4):
                        swap_quarter(nxt, 3, quarter)
                exps(1, 4, 12)
                if more:
                    round_group(nxt, 3)

            head_squares(PAIRS - 1)

            def take_z(p, t):
                n = p * 8 + t
                if n - 1 > 0:
                    act.wait_ge(y_ready, n - 1)
                act.activation(silu[:, n % 2, :], bank[:, t, :],
                               ACT.Silu).then_inc(bank_free, 1)
            panel_stage(2, FIRST_Z, 2, take_z)
            split_hi(FIRST_O0, FIRST_O0 + 3)
            for m in range(2):
                for t in range(NT):
                    turn_hi(1, 8 * m + t, t, m)

            def residual_squares(first_panel, first_chunk, src, junk):
                split_hi(first_chunk + 3, first_chunk + NK + 3)
                for t in range(NT):
                    half_squares(first_panel, src, junk, 0, t)
                split_hi(first_chunk + NK + 3, first_chunk + 2 * NK)
            residual_squares(4, FIRST_O0, buf[1], buf[0])
            for t in range(NT + 4):
                if t < NT:
                    half_squares(4, buf[1], buf[0], 1, t)
                if 2 <= t < NT + 2:
                    scale_half(1, buf[0], t - 2)
                if t >= 4:
                    for m in range(2):
                        turn_hi(2, 2 * (t - 4) + m, t - 4, m)
            split_hi(FIRST_A, FIRST_A + 3)
            split_hi(FIRST_A + 3, FIRST_A + 4)
            act.wait_ge(gate_e, 2)
            act.activation(gr[1][:], gr[1][:], ACT.Exp, scale=-1.0).then_inc(gate_exp, 1)
            act.wait_ge(gate_exp, 2)
            act.activation(gr[1][:], gr[1][:], ACT.Ln, bias=1.0).then_inc(gate_ln, 1)

            def take_a(p, t):
                if p < 2:
                    dst = qk_rows[:, t, p * PANEL:(p + 1) * PANEL]
                    src = bank[:, t, :]
                else:
                    dst = v_rows[:, t, 4 * (p - 2):4 * (p - 1), 0:P]
                    src = bank[:, t, :].rearrange("p (h e) -> p h e", h=4)
                act.activation(dst, src, ACT.Copy).then_inc(bank_free, 1)
            act.wait_ge(x1_stored, 16 * NT)
            panel_stage(6, FIRST_A, 4, take_a, split=4)

            def take_b(p, t):
                if p < 2:
                    act.activation(gl_rows[:, t, p * PANEL:(p + 1) * PANEL], bank[:, t, :],
                                   ACT.Sigmoid).then_inc(bank_free, 1)
                else:
                    n = (p - 2) * 8 + t
                    if n - 1 > 0:
                        act.wait_ge(gl_ready, n - 1)
                    act.activation(zs[:, n % 2, :], bank[:, t, :],
                                   ACT.Silu).then_inc(bank_free, 1)
            split_hi(FIRST_B, FIRST_B + 3)
            for b in range(2):
                act.wait_ge(cols_turned, b + 1)
                src = bank[:, b, 0:416].rearrange("p (c k e) -> p c k e", c=4, k=13)
                act.activation(cols[:, 4 * b:4 * b + 4, 0, :], src[:, :, 0, :], ACT.Copy)
                for kind in range(1, 4):
                    last = act.activation(cols[:, 4 * b:4 * b + 4, kind, :], src[:, :, 4 * kind, :], ACT.Exp)
                last.then_inc(cols_ready, 1)
            act.wait_ge(wold_bc, 1)
            src = bank[:, 2, 0:NT * ML_HEADS].rearrange("p (c m r) -> p c m r", c=NT, r=2)
            act.activation(w_old[0:64, :, 0:4], src[0:64, :, :, 0], ACT.Exp)
            act.activation(w_old[64:128, :, 0:4], src[64:128, :, :, 1], ACT.Exp).then_inc(cols_ready, 1)

            def cell_decay(c):
                act.wait_ge(mask_ready, c + 1)
                for h in range(ML_HEADS):
                    d = decay[c % 3][:, h, :]
                    last = act.activation(d, d, ACT.Exp, bias=cols[:, c, 0, h:h + 1])
                last.then_inc(d_ready, 1)
            split_hi(FIRST_B + 3, FIRST_B + 4)
            cell_decay(0)
            cell_decay(1)
            act.wait_ge(m_stored, 16)
            panel_stage(10, FIRST_B, 4, take_b, split=4)
            split_hi(FIRST_O1, FIRST_O1 + 3)

            def cell_q(c):
                act.wait_ge(q_turned, c + 1)
                if c > 1:
                    act.wait_ge(s_in, 2 * (c - 1))
                act.activation(q_t[c % 2][:], bank[:, 0, :].rearrange("p (m c) -> p m c", m=4), ACT.Copy,
                               scale=ML_QK ** -0.5).then_inc(q_ready, 1)
                act.wait_ge(k_turned, c + 1)
                act.activation(k_t[c % 2][:], bank[:, 1, :].rearrange("p (m c) -> p m c", m=4),
                               ACT.Copy).then_inc(k_ready, 1)

            def cell_decayed(c):
                act.wait_ge(qd_turned, c + 1)
                if c > 1:
                    act.wait_ge(inter_in, 2 * (c - 1))
                act.activation(qd_t[c % 2][:], bank[:, 0, :].rearrange("p (m c) -> p m c", m=4), ACT.Copy,
                               scale=ML_QK ** -0.5).then_inc(qd_copied, 1)

            cell_q(0)
            cell_decayed(0)
            for c in range(NT):
                if c + 1 < NT:
                    cell_q(c + 1)
                if c + 2 < NT:
                    cell_decay(c + 2)
                if c + 1 < NT:
                    cell_decayed(c + 1)
            act.wait_ge(state_ready, 2 * NT)
            for t in range(NT):
                for m in range(2):
                    turn_hi(3, 2 * t + m, t, m)
            residual_squares(14, FIRST_O1, buf[0], buf[1])
            for t in range(NT + 2):
                if t < NT:
                    half_squares(14, buf[0], buf[1], 1, t)
                if t >= 2:
                    scale_half(2, buf[1], t - 2)

        @block.vector
        def _(dve):
            steps = [0]

            def step(ins):
                steps[0] += 1
                ins.then_inc(dve_chain, 1)
                dve.wait_ge(dve_chain, steps[0])

            V = nc.vector

            def split_lo(lo, hi):
                for n in range(lo, hi):
                    dve.wait_ge(hi_split, n + 1)
                    V.tensor_tensor(w_lo[:, n % RING, :], w_raw[:, n % RING, :],
                                    w_hi[:, n % RING, :].bitcast(F32), ALU.subtract).then_inc(w_ready, 1)

            def turn_lo(stage, n, t, m):
                dve.wait_ge(turned_hi, 16 * stage + n + 1)
                V.tensor_tensor(ht_lo[:, 4 * m:4 * m + 4, t * P:(t + 1) * P],
                                bank[:, n % 8, :].rearrange("p (k c) -> p k c", k=4),
                                ht_hi[:, 4 * m:4 * m + 4, t * P:(t + 1) * P].bitcast(F32),
                                ALU.subtract).then_inc(turned_lo, 1)

            def normalise(n, src, dst, t):
                dve.wait_ge(rstd_ready, NT * n + t + 1)
                V.scalar_tensor_tensor(out=dst[:, t, :], in0=src[:, t, :], scalar=stat[:, 2, t:t + 1],
                                       in1=g_rows[:], op0=ALU.mult, op1=ALU.mult).then_inc(xn_ready, 1)

            def normalise_half(n, src, dst, t):
                dve.wait_ge(rstd_ready, NT * n + t + 1)
                V.scalar_tensor_tensor(out=dst[:, t, PANEL:], in0=src[:, t, PANEL:], scalar=stat[:, 2, t:t + 1],
                                       in1=g_rows[:, PANEL:], op0=ALU.mult, op1=ALU.mult).then_inc(xn_ready, 1)

            def premultiply(n, src, dst, t):
                dve.wait_ge(squares_ready, squares_of(n, t) - NT)
                V.tensor_tensor(dst[:, t, 0:PANEL], src[:, t, 0:PANEL], g_rows[:, 0:PANEL],
                                ALU.mult).then_inc(xg_ready, 1)

            def split_gates(w):
                step(V.tensor_copy(gate_hi[:, :, 0:w], gate_raw[:, :, 0:w]))
                V.tensor_tensor(gate_lo[:, :, 0:w], gate_raw[:, :, 0:w], gate_hi[:, :, 0:w].bitcast(F32),
                                ALU.subtract).then_inc(gate_split, 1)

            def panel_stage(first_panel, first_chunk, n, take=None, split=3):
                for p in range(n):
                    c = first_chunk + NK * p
                    split_lo(c + (split if p == 0 else 3), c + NK)
                    if p + 1 < n:
                        split_lo(c + NK, c + NK + 3)
                    for t in range(NT if take else 0):
                        dve.wait_ge(acc_ready, 8 * (first_panel + p) + t + 1)
                        take(p, t)

            def log_gate(u, a, src, bias, n):
                V.tensor_scalar(u, src, bias, None, ALU.add).then_inc(gate_u, 1)
                dve.wait_ge(gate_u, n)
                V.scalar_tensor_tensor(out=a, in0=u, scalar=-1.0, in1=u, op0=ALU.mult,
                                       op1=ALU.max).then_inc(gate_e, 1)
                dve.wait_ge(gate_ln, n)
                step(V.scalar_tensor_tensor(out=u, in0=u, scalar=0.0, in1=a, op0=ALU.min, op1=ALU.subtract))

            dve.wait_ge(consts_loaded, 16)
            for dst, c in ((ident, C_IDENT), (ident_r, C_IDENT),
                           (mask_q, C_MASKQ), (mask_k, C_MASKK)):
                V.tensor_copy(dst[:], c_raw[:, c:c + P])
            V.tensor_copy(inv_sign[:], c_raw[:, C_INV:C_INV + 2]).then_inc(consts_ready, 1)
            dve.wait_ge(consts_ready, 1)
            dve.wait_ge(lam_loaded, 16)
            pairs_l = lam_row[:, 0:4 * HEAD_DIM].rearrange("p (a b c) -> p a b c", a=2, b=2)
            step(V.tensor_tensor(pairs_l[:, :, 0, :], pairs_l[:, :, 0, :], pairs_l[:, :, 1, :], ALU.mult))
            V.tensor_reduce(lam_row[:, 256:258], pairs_l[:, :, 0, :], AX.X, ALU.add).then_inc(lam_sum, 1)
            dve.wait_ge(lam_sum, 1)
            dve.wait_ge(lam_exp, 1)
            step(V.tensor_tensor(lam_row[:, 260:261], lam_row[:, 258:259], lam_row[:, 259:260], ALU.subtract))
            step(V.tensor_scalar(lam_row[:, 261:262], lam_row[:, 260:261], -1.0, -LAM_INIT, ALU.mult, ALU.add))
            V.memset(lam_row[:, 0:P], 1.0).then_inc(lam_one, 1)
            dve.wait_ge(g_loaded, 16)
            for t in range(NT + 3):
                if t < NT:
                    normalise(0, buf[0], buf[1], t)
                if t == 7:
                    dve.wait_ge(small_loaded, 64)
                    split_gates(8)
                if t >= 3:
                    for m in range(2):
                        turn_lo(0, 2 * (t - 3) + m, t - 3, m)
            split_lo(FIRST_V, FIRST_V + 3)
            dve.wait_ge(lam_bc, 1)
            V.tensor_copy(neg_lam[:], bank[:, 2, 0:1]).then_inc(lam_ready, 1)
            dve.wait_ge(gate_acc, 2)
            log_gate(row[0][:].rearrange("p (a b) -> p a b", a=2), row[1][:].rearrange("p (a b) -> p a b", a=2),
                     bank[0:8, 0:2, :], gate_b[:, 0:1], 1)
            step(V.memset(f_parts[:, 0, :].bitcast(F32), 1.0))
            step(V.tensor_tensor_scan(row[1][:], f_parts[:, 0, :].bitcast(F32), row[0][:], 0.0, ALU.mult, ALU.add))
            step(V.tensor_scalar(f_parts[:, 0, :], row[1][:], -8.0, None, ALU.mult))
            V.scalar_tensor_tensor(out=f_parts[:, 1, :], in0=row[1][:], scalar=-8.0,
                                   in1=f_parts[:, 0, :].bitcast(F32), op0=ALU.mult,
                                   op1=ALU.subtract).then_inc(f_ready, 1)
            split_lo(FIRST_V + 3, FIRST_V + 4)
            dve.wait_ge(pos_loaded, 16)
            step(V.tensor_copy(turn[:], pos_i[:]))
            step(V.tensor_scalar(angle[:], turn[:], inv_sign[:, 0:1], None, ALU.mult))
            step(V.tensor_scalar(turn[:], angle[:], 1.0 / (2.0 * math.pi), ROUND, ALU.mult, ALU.add))
            step(V.tensor_scalar(turn[:], turn[:], ROUND, None, ALU.subtract))
            split_lo(FIRST_V + 4, FIRST_V + 5)
            for part in (TWO_PI_1, TWO_PI_2, TWO_PI_3):
                step(V.scalar_tensor_tensor(out=angle[:], in0=turn[:], scalar=-part, in1=angle[:],
                                            op0=ALU.mult, op1=ALU.add))
            step(V.tensor_scalar(angle[:], angle[:], PI_SAFE, -PI_SAFE, ALU.min, ALU.max))
            step(V.scalar_tensor_tensor(out=turn[:], in0=angle[:], scalar=-1.0, in1=angle[:],
                                        op0=ALU.mult, op1=ALU.max))
            V.tensor_scalar(turn[:], turn[:], -1.0, math.pi / 2, ALU.mult,
                            ALU.add).then_inc(rope_args, 1)
            split_lo(FIRST_V + 5, FIRST_V + 7)
            dve.wait_ge(turned, 16)
            for c in range(2):
                for a in range(2):
                    V.memset(q_b[c][a][64:68, :].bitcast(F32), 1.0)
                    V.memset(k_b[c][a][64:68, :].bitcast(F32), 1.0)
                last = V.memset(v_pair[c][:], 1.0)
            last.then_inc(helper_init, 1)
            V.tensor_scalar(sub_g[:], sub_g[:], 1.0 - LAM_INIT, None, ALU.mult).then_inc(helper_sub, 1)
            dve.wait_ge(rope_ready, 1)
            step(V.tensor_scalar(sin_t[:], sin_t[:], inv_sign[:, 1:2], None, ALU.mult))
            panel_stage(0, FIRST_V, 2, split=7)
            split_lo(FIRST_PAIRS, FIRST_PAIRS + 4)

            def lo_group(u, g):
                kind, half = u % 2, slice((g % 2) * PANEL, (g % 2 + 1) * PANEL)
                dve.wait_ge(qk_hi, 2 * (4 * u + g + 1))
                for a in range(2):
                    r, other = slice(64 * a, 64 * a + 64), slice(64 - 64 * a, 128 - 64 * a)
                    src = rot[r, :] if kind else bank[r, g % 2, :]
                    if g < 2:
                        hi, dst = q_a[kind][a][r, half], q_b[kind][a][0:64, half]
                    else:
                        hi, dst = k_a[kind][a][r, half], k_a[kind][a][other, half]
                    last = V.tensor_tensor(dst, src, hi.bitcast(F32), ALU.subtract)
                last.then_inc(qk_ready, 1)

            def rope(u, g):
                n = 4 * (u // 2) + g + 1
                dve.wait_ge(pj_copied, 4 * n)
                dve.wait_ge(qk_ready, 4 * u + g)
                half = slice((g % 2) * PANEL, (g % 2 + 1) * PANEL)
                V.tensor_tensor(rot[:], bank[:, g % 2, :], cos_t[:, half], ALU.mult).then_inc(pj_free, 1)
                step(V.tensor_tensor(qs[:], qs[:], sin_t[:, half], ALU.mult))
                dve.wait_ge(pj_free, n)
                V.tensor_tensor(rot[:], rot[:], qs[:], ALU.add).then_inc(roped, 1)

            for t in range(NT):
                dve.wait_ge(v_stored[t], 32)
            for g in range(4):
                lo_group(0, g)

            for u in range(PAIRS):
                kind, nxt = u % 2, u + 1
                more, after = nxt < PAIRS, u + 2 < PAIRS
                turn_n = nxt % 2 == 1

                def maxima(a, lo, hi):
                    for n in range(lo, hi):
                        w = MAX_CHUNKS[n][2]
                        dve.wait_ge(max_in, 24 * u + 12 * a + n + 1)
                        V.tensor_reduce(m_part[:, a, n:n + 1], bank[:, 2 + n % 4, 0:w * P], AX.X,
                                        ALU.max).then_inc(max_done, 1)

                def negate_maximum(a):
                    dve.wait_ge(max_done, 24 * u + 12 * a + 12)
                    step(V.tensor_copy(m_max[:, a, 0:4], m_part[:, a, 0:4]))
                    step(V.tensor_tensor(m_max[:, a, 4:8], m_part[:, a, 4:12:2], m_part[:, a, 5:12:2], ALU.max))
                    step(V.tensor_scalar(m_cols[:, a, 0, :], m_max[:, a, :], -1.0, None, ALU.mult))
                    V.scalar_tensor_tensor(out=m_cols[:, a, 1, :], in0=m_max[:, a, :], scalar=-1.0,
                                           in1=m_cols[:, a, 0, :].bitcast(F32), op0=ALU.mult,
                                           op1=ALU.subtract).then_inc(m_ready, 1)

                def maximum_rows(a):
                    dve.wait_ge(m_turned, 2 * u + a + 1)
                    if u > 0:
                        dve.wait_ge(m_moved[a], 32 * u)
                    V.tensor_copy(m_rows[:, a, :], bank[0:2 * NT, 6 + a, 3 * P:4 * P]).then_inc(m_copied, 1)

                def outputs(a, lo, hi):
                    width = 65 if kind == 0 else 129
                    for b in range(lo, hi):
                        dve.wait_ge(pv_ready, 8 * u + 4 * a + b + 1)
                        at = slice(8 * a + 2 * b, 8 * a + 2 * b + 2)
                        pv = bank[:, 6 + b % 2, 0:2 * width].rearrange("p (i e) -> p i e", i=2)
                        values = pv[:, :, 0:width - 1]
                        tiles = slice(2 * b, 2 * b + 2)
                        step(V.reciprocal(recip[:, 0, at], pv[:, :, width - 1]))
                        if a == 1 and kind == 1:
                            step(V.tensor_scalar(recip[:, 1, at], recip[:, 0, at], neg_lam[:, 0:1], None, ALU.mult))
                            for i in range(2):
                                n, m = 2 * b + i, 8 * a + 2 * b + i
                                last = V.scalar_tensor_tensor(out=o_pair[1][:, n, :], in0=values[:, i, :],
                                                              scalar=recip[:, 1, m:m + 1],
                                                              in1=o_pair[1][:, n, :], op0=ALU.mult, op1=ALU.add)
                        else:
                            dst = o_pair[kind][:, tiles, 64 * a:64 * a + 64] if kind == 0 else o_pair[1][:, tiles, :]
                            last = V.tensor_tensor(dst, values, recip[:, 0, at].unsqueeze(2).broadcast_to(
                                [P, 2, width - 1]), ALU.mult)
                        last.then_inc(pv_free, 1)

                if u == 0:
                    split_lo(FIRST_PAIRS + 4, FIRST_PAIRS + 6)
                maxima(0, 0, 6)
                if more:
                    split_lo(FIRST_PAIRS + 4 * nxt + 2, FIRST_PAIRS + 4 * nxt + 4)
                maxima(0, 6, 12)
                negate_maximum(0)
                maxima(1, 0, 4)
                if more and not turn_n:
                    lo_group(nxt, 0)
                maxima(1, 4, 6)
                maximum_rows(0)
                maxima(1, 6, 9)
                if more and turn_n:
                    rope(nxt, 0)
                maxima(1, 9, 12)
                negate_maximum(1)
                maximum_rows(1)
                if more and turn_n:
                    lo_group(nxt, 0)
                    rope(nxt, 1)
                if more:
                    lo_group(nxt, 1)
                if u // 2 > 0:
                    dve.wait_ge(o_stored[kind], 16 * (u // 2))
                if u > 0:
                    dve.wait_ge(pv_free, 8 * u)
                outputs(0, 0, 2)
                if more and turn_n:
                    rope(nxt, 2)
                if more:
                    lo_group(nxt, 2)
                outputs(0, 2, 4)
                if after:
                    split_lo(FIRST_PAIRS + 4 * (u + 2), FIRST_PAIRS + 4 * (u + 2) + 2)
                if u == PAIRS - 1:
                    split_lo(FIRST_Z, FIRST_Z + 3)
                if more and turn_n:
                    rope(nxt, 3)
                outputs(1, 0, 2)
                if more:
                    lo_group(nxt, 3)
                outputs(1, 2, 4)

            def gate_outputs(p, t):
                dve.wait_ge(o_loaded[t], 16)
                dve.wait_ge(bank_free, taken(2 + p, t))
                d = buf[0][:, t, p * PANEL:(p + 1) * PANEL]
                V.tensor_tensor(d, d, silu[:, t % 2, :], ALU.mult).then_inc(y_ready, 1)
            panel_stage(2, FIRST_Z, 2, gate_outputs)
            split_lo(FIRST_O0, FIRST_O0 + 3)
            for m in range(2):
                for t in range(NT):
                    turn_lo(1, 8 * m + t, t, m)

            def residual(dst, arrived, count, first_panel, p, t):
                dve.wait_ge(arrived[t], count)
                dve.wait_ge(acc_ready, 8 * (first_panel + p) + t + 1)
                d = dst[:, t, p * PANEL:(p + 1) * PANEL]
                V.tensor_tensor(d, bank[:, t, :], d, ALU.add).then_inc(bank_free, 1)

            def first_residual(n, dst, scaled, arrived, count, first_panel, first_chunk, g_arrived, g_count):
                split_lo(first_chunk + 3, first_chunk + NK + 3)
                for t in range(NT):
                    residual(dst, arrived, count, first_panel, 0, t)
                dve.wait_ge(g_arrived, g_count)
                for t in range(NT):
                    premultiply(n, dst, scaled, t)
                split_lo(first_chunk + NK + 3, first_chunk + 2 * NK)
            first_residual(1, buf[1], buf[0], x_again, 16, 4, FIRST_O0, g1_loaded, 32)
            split_gates(16)
            for t in range(NT + 5):
                if t < NT:
                    residual(buf[1], x_again, 16, 4, 1, t)
                if 2 <= t < NT + 2:
                    normalise_half(1, buf[1], buf[0], t - 2)
                if t >= 5:
                    for m in range(2):
                        turn_lo(2, 2 * (t - 5) + m, t - 5, m)
            split_lo(FIRST_A, FIRST_A + 3)

            dve.wait_ge(gate_acc, 4)
            V.tensor_copy(g_in[:].rearrange("p (a b) -> p a b", a=2), bank[0:16, 0:2, :]).then_inc(gate_in, 1)
            dve.wait_ge(ml_loaded, 16)
            dve.wait_ge(gate_moved, 16)
            fg, tmp, b_row, u_row, m_row = (g[:] for g in gr)

            def chunks(r):
                return r.rearrange("p (c t) -> p c t", c=NT)
            split_lo(FIRST_A + 3, FIRST_A + 4)
            log_gate(fg, tmp, fg, gate_b[:, 2:3], 2)
            step(V.tensor_tensor_scan(b_row, reset[:], fg, 0.0, ALU.mult, ALU.add))
            step(V.scalar_tensor_tensor(out=u_row, in0=g_in[0:8, :], scalar=gate_b[:, 1:2], in1=b_row,
                                        op0=ALU.add, op1=ALU.subtract))
            split_lo(FIRST_A + 4, FIRST_A + 5)
            step(V.memset(tmp, 0.0))
            step(V.tensor_copy(chunks(tmp)[:, 1:NT, 0], chunks(b_row)[:, 0:NT - 1, P - 1]))
            step(V.tensor_tensor_scan(m_row, tmp, u_row, 0.0, ALU.add, ALU.max))
            V.tensor_scalar(tmp, m_row, -1.0, None, ALU.mult).then_inc(neg_ready, 1)
            split_lo(FIRST_A + 5, FIRST_A + 6)
            step(V.memset(lrow[:], 0.0))
            step(V.tensor_tensor(lrow[:, 1:NT, 8], chunks(m_row)[:, 0:NT - 1, P - 1],
                                 chunks(b_row)[:, 0:NT - 1, P - 1], ALU.add))
            step(V.tensor_tensor(lrow[:, :, 9], lrow[:, :, 8], chunks(m_row)[:, :, P - 1], ALU.subtract))
            step(V.tensor_tensor(lrow[:, :, 0:8], lrow[:, :, 9:10].broadcast_to([8, NT, 8]),
                                 ident[0:8, 0:8].unsqueeze(1).broadcast_to([8, NT, 8]), ALU.mult))
            step(V.memset(rows4[:], 0.0))
            V.tensor_copy(rows4[0:8, :], u_row)
            V.tensor_tensor(chunks(rows4[32:40, :]), lrow[:, :, 8:9].broadcast_to([8, NT, P]), chunks(m_row),
                            ALU.subtract)
            V.scalar_tensor_tensor(out=rows4[64:72, :], in0=b_row, scalar=-1.0, in1=m_row, op0=ALU.mult,
                                   op1=ALU.subtract)
            V.tensor_tensor(chunks(rows4[96:104, :]), chunks(u_row),
                            chunks(m_row)[:, :, P - 1:P].broadcast_to([8, NT, P]), ALU.subtract)
            V.memset(ones8[:], 1.0).then_inc(gate_l, 1)
            split_lo(FIRST_A + 6, FIRST_A + 7)
            dve.wait_ge(x1_stored, 16 * NT)
            V.memset(v_rows[:, :, :, P:P + 2], 1.0)
            panel_stage(6, FIRST_A, 4, split=7)
            split_lo(FIRST_B, FIRST_B + 3)

            def gate_product(p, t):
                if p >= 2:
                    dve.wait_ge(bank_free, taken(10 + p, t))
                    d = gl_rows[:, t, (p - 2) * PANEL:(p - 1) * PANEL]
                    V.tensor_tensor(d, d, zs[:, t % 2, :], ALU.mult).then_inc(gl_ready, 1)

            panel_stage(10, FIRST_B, 4, gate_product)
            split_lo(FIRST_O1, FIRST_O1 + 3)
            dve.wait_ge(acc_ready, 8 * 14)
            V.memset(state[:], 0.0).then_inc(ml_init, 1)

            def cell_sd(c):
                dve.wait_ge(d_ready, c + 1)
                for r in range(2):
                    dve.wait_ge(s_in, 2 * c + r + 1)
                    if c > 1:
                        dve.wait_ge(inter_in, 2 * (c - 1))
                    V.tensor_tensor(sd[2 * (c % 2) + r][:], bank[:, 2 + r, :].rearrange("p (h t) -> p h t", h=4),
                                    decay[c % 3][:, r:8:2, :], ALU.mult).then_inc(sd_ready, 1)

            def cell_take(c, mm):
                dve.wait_ge(inter_in, 2 * c + mm + 1)
                num = bank[:, 4 + 2 * mm:6 + 2 * mm, 0:258].rearrange("p r (i e) -> p r i e", i=2)
                floor = cols[:, c, 2, 4 * mm:4 * mm + 4].rearrange("p (i r) -> p r i", r=2)
                step(V.tensor_scalar(den[:, mm, 0], num[:, :, :, P], -1.0, None, ALU.mult))
                step(V.tensor_tensor(den[:, mm, 1], num[:, :, :, P], den[:, mm, 0], ALU.max))
                step(V.tensor_tensor(den[:, mm, 2], den[:, mm, 1], floor, ALU.max))
                step(V.reciprocal(den[:, mm, 0], den[:, mm, 2]))
                for i in range(2):
                    V.scalar_tensor_tensor(out=state[:, 2 * mm + i, 0:129], in0=state[:, 2 * mm + i, 0:129],
                                           scalar=w_old[:, c, 2 * mm + i:2 * mm + i + 1],
                                           in1=bank[:, 4 + 2 * mm + i, 258:387], op0=ALU.mult, op1=ALU.add)
                for i in range(2):
                    for r in range(2):
                        h = 4 * mm + 2 * i + r
                        y = gl_rows[:, c, h * P:(h + 1) * P]
                        last = V.scalar_tensor_tensor(out=y, in0=num[:, r, i, 0:P], scalar=den[:, mm, 0, r, i:i + 1],
                                                      in1=y, op0=ALU.mult, op1=ALU.mult)
                last.then_inc(state_ready, 1)

            cell_sd(0)
            for c in range(NT):
                cell_take(c, 0)
                if c + 1 < NT:
                    cell_sd(c + 1)
                cell_take(c, 1)
            for t in range(NT):
                for m in range(2):
                    turn_lo(3, 2 * t + m, t, m)
            first_residual(2, buf[0], buf[1], tile_loaded, 32, 14, FIRST_O1, g2_loaded, 16)
            for t in range(NT + 2):
                if t < NT:
                    residual(buf[0], tile_loaded, 32, 14, 1, t)
                if t >= 2:
                    normalise_half(2, buf[0], buf[1], t - 2)

        @block.gpsimd
        def _(pool):
            G = nc.gpsimd
            steps = [0]

            def step(ins):
                steps[0] += 1
                ins.then_inc(pool_chain, 1)
                pool.wait_ge(pool_chain, steps[0])


            def rstd(n, parts):
                for t in range(NT):
                    pool.wait_ge(squares_ready, squares_of(n, t))
                    if parts == 2:
                        step(G.tensor_tensor(stat[:, 0, t:t + 1], stat[:, 0, t:t + 1], stat[:, 3, t:t + 1], ALU.add))
                    G.tensor_scalar(stat[:, 1, t:t + 1], stat[:, 0, t:t + 1], 1.0 / D_MODEL, EPS, ALU.mult,
                                    ALU.add).then_inc(mean_ready, 1)
                    pool.wait_ge(mean_ready, NT * n + t + 1)
                    G.tensor_tensor(stat[:, 2, t:t + 1], stat[:, 1, t:t + 1], neg_half[:, 0:1],
                                    ALU.pow).then_inc(rstd_ready, 1)

            step(G.memset(neg_half[:], -0.5))
            rstd(0, 1)
            pool.wait_ge(f_ready, 1)
            pool.dma_start(f_scr, f_parts[:]).then_inc(f_stored, 16)
            for p in range(2):
                for t in range(NT):
                    pool.wait_ge(bank_free, taken(p, t))
                    pool.dma_start(v_scr[t * P:(t + 1) * P, p * PANEL:(p + 1) * PANEL],
                                   v_stage[:, t, :]).then_inc(v_stored[t], 16)

            def move_maximum(u, a):
                at = 66 - 2 * (u % 2)
                pool.wait_ge(m_copied, 2 * u + a + 1)
                for j in range(2):
                    pool.dma_start(q_b[u % 2][a][at + j:at + j + 1, :].rearrange("p (t c) -> p t c", t=NT),
                                   m_rows[NT * j:NT * j + NT, a, :]).then_inc(m_moved[a], 16)

            def load_pair(u):
                kind, j = u % 2, u // 2
                src = v_scr.rearrange("(t p) d -> p t d", p=P)
                if kind:
                    pool.dma_start(v_pair[1][:, :, 0:P],
                                   src[:, :, FOX_WIDTH + P * j:FOX_WIDTH + P * (j + 1)]).then_inc(v_loaded[1], 16)
                else:
                    for a in range(2):
                        pool.dma_start(v_pair[0][:, :, 65 * a:65 * a + 64],
                                       src[:, :, P * j + 64 * a:P * j + 64 * a + 64]).then_inc(v_loaded[0], 16)

            def load_rowf(u):
                for a in range(2):
                    pool.dma_start(k_b[0][a][64:66, :], f_scr[u + a]).then_inc(rowf_loaded, 16)

            for t in range(NT):
                pool.wait_ge(v_stored[t], 32)
            pool.wait_ge(helper_init, 1)
            pool.wait_ge(helper_sub, 1)
            pool.wait_ge(f_stored, 16)

            def twice(u, g):
                kind, half = u % 2, slice((g % 2) * PANEL, (g % 2 + 1) * PANEL)
                for a in range(2):
                    r, other = slice(64 * a, 64 * a + 64), slice(64 - 64 * a, 128 - 64 * a)
                    pool.wait_ge(qk_hi, 2 * (4 * u + g) + a + 1)
                    if g < 2:
                        src, dst = q_a[kind][a][r, half], q_a[kind][a][other, half]
                    else:
                        src, dst = k_a[kind][a][r, half], k_b[kind][a][0:64, half]
                    G.tensor_copy(dst, src).then_inc(qk_twice, 1)
                    pool.wait_ge(qk_twice, 2 * (4 * u + g) + a + 1)

            load_rowf(0)
            load_pair(0)
            o_rows = o_scr.rearrange("(t p) d -> p t d", p=P)
            for u in range(PAIRS):
                kind, j = u % 2, u // 2
                if u + 1 < PAIRS:
                    if u > 0:
                        pool.wait_ge(pv_ready, 8 * u)
                    load_pair(u + 1)
                    if kind:
                        load_rowf(u + 1)
                move_maximum(u, 0)
                if u + 1 < PAIRS:
                    twice(u + 1, 0)
                move_maximum(u, 1)
                if u + 1 < PAIRS:
                    for g in range(1, 4):
                        twice(u + 1, g)
                pool.wait_ge(pv_free, 8 * (u + 1))
                o = o_pair[kind]
                if kind:
                    pool.wait_ge(o_squares, NT * (j + 1))
                    step(G.tensor_scalar(sub_ss[:, 1, :], sub_ss[:, 0, :], 1.0 / P, EPS, ALU.mult, ALU.add))
                    step(G.tensor_tensor(sub_ss[:, 0, :], sub_ss[:, 1, :], neg_half[:], ALU.pow))
                    step(G.tensor_tensor(o[:], o[:], sub_ss[:, 0, :].unsqueeze(2).broadcast_to([P, NT, P]), ALU.mult))
                    step(G.tensor_tensor(o[:], o[:], sub_g[:].unsqueeze(1).broadcast_to([P, NT, P]), ALU.mult))
                pool.dma_start(o_rows[:, :, FOX_WIDTH * kind + P * j:FOX_WIDTH * kind + P * (j + 1)],
                               o[:]).then_inc(o_stored[kind], 16)

            for c in range(2):
                pool.wait_ge(o_stored[c], 16 * PAIRS // 2)
            for t in range(NT):
                pool.dma_start(buf[0][:, t, :], o_scr[t * P:(t + 1) * P, :]).then_inc(o_loaded[t], 16)
            rstd(1, 2)

            def cell_mask(c):
                pool.wait_ge(m_loaded[c % 3], 16 * (c // 3 + 1))
                G.tensor_tensor(decay[c % 3][:], decay[c % 3][:],
                                mask_k[:].bitcast(F32).unsqueeze(1).broadcast_to([P, ML_HEADS, P]),
                                ALU.add).then_inc(mask_ready, 1)

            def cell_weighted(c):
                if c > 0:
                    pool.wait_ge(qd_turned, c)
                G.tensor_tensor(q_decayed[:], qk_rows[:, c, 0:PANEL].rearrange("p (h d) -> p h d", h=8),
                                cols[:, c, 1, :].unsqueeze(2).broadcast_to([P, 8, ML_QK]),
                                ALU.mult).then_inc(qd_ready, 1)
                if c > 1:
                    pool.wait_ge(inter_in, 2 * (c - 1))
                G.tensor_tensor(kw[c % 2][:], qk_rows[:, c, PANEL:2 * PANEL].rearrange("p (h d) -> p h d", h=8),
                                cols[:, c, 3, :].unsqueeze(2).broadcast_to([P, 8, ML_QK]),
                                ALU.mult).then_inc(kw_ready, 1)

            pool.wait_ge(neg_ready, 1)
            pool.dma_start(m_scr, gr[1][:]).then_inc(m_stored, 16)
            pool.wait_ge(cols_ready, 3)
            cell_mask(0)
            cell_mask(1)
            pool.wait_ge(acc_ready, 8 * 14)
            cell_weighted(0)
            for c in range(NT):
                if c + 1 < NT:
                    cell_weighted(c + 1)
                if c + 2 < NT:
                    cell_mask(c + 2)
            rstd(2, 2)


def kernel(x, positions, attn_norm_g, attn_w_in, fox_b_f, diff_lam_q1, diff_lam_k1, diff_lam_q2, diff_lam_k2,
           diff_subln_g, attn_w_out, ml_norm_g, ml_w_in, ml_b_i, ml_b_f, ml_w_out, final_norm_g):
    import concourse.bacc as bacc
    from concourse.bass_utils import run_bass_kernel_spmd

    arrays = {
        "x": x, "positions": positions, "attn_norm_g": attn_norm_g, "attn_w_in": attn_w_in, "fox_b_f": fox_b_f,
        "lams": np.concatenate([np.asarray(a) for a in (diff_lam_q1, diff_lam_k1, diff_lam_q2, diff_lam_k2)], axis=1),
        "subln_g": diff_subln_g, "attn_w_out": attn_w_out, "ml_norm_g": ml_norm_g, "ml_w_in": ml_w_in,
        "ml_b": np.concatenate([np.asarray(ml_b_i), np.asarray(ml_b_f)], axis=0).T, "ml_w_out": ml_w_out,
        "final_norm_g": final_norm_g, "const": constants(),
    }
    arrays = {"in_" + k: np.ascontiguousarray(v) for k, v in arrays.items()}
    nc = bacc.Bacc("TRN2", target_bir_lowering=False, num_devices=1)
    args = [nc.dram_tensor(k, v.shape, mybir.dt.from_np(v.dtype), kind="ExternalInput").ap()
            for k, v in arrays.items()]
    args.append(nc.dram_tensor("out_y", (1, SEQ, D_MODEL), F32, kind="ExternalOutput").ap())
    build(nc, *args)
    return run_bass_kernel_spmd(nc, [arrays], core_ids=[0]).results[0]["out_y"]
```
